# Optimizing a Trainium2 kernel written in Bass

```python
import numpy as np
import jax
import jax.numpy as jnp
from jax import lax

D_MODEL = 1024
BATCH = 1
SEQ = 512
DEPTH = 2

HEAD_DIM = 64
D_MIX = D_MODEL
N_META = 16
BLOCK = 128
PAD = BLOCK - N_META
ROPE_THETA = 500000.0
ROPE_DIM = HEAD_DIM // 4
NEG = -1e30

DSA_HEADS = 4
IDX_HEADS = 4
IDX_DIM = 64
TOPK_MAX = 256

FOX_HEADS = 4

GLA_HEADS = 4
GLA_DK = 64
GLA_DV = 128
GLA_RANK = 16
GLA_TAU = 16.0
GLA_CHUNK = 64

D_FF = ((8 * D_MODEL + 3 * 256 - 1) // (3 * 256)) * 256

IN_SPLITS = (
    DSA_HEADS * HEAD_DIM, HEAD_DIM, HEAD_DIM,
    IDX_HEADS * IDX_DIM, IDX_HEADS, IDX_DIM,
    FOX_HEADS * HEAD_DIM, FOX_HEADS * HEAD_DIM, FOX_HEADS * HEAD_DIM, FOX_HEADS,
    GLA_HEADS * GLA_DK, GLA_HEADS * GLA_DK, GLA_HEADS * GLA_DV, GLA_HEADS * GLA_DV, GLA_RANK,
)
N_IN = sum(IN_SPLITS)

kernel_name = 'hybrid_dsa_fox_gla_block'

def rms_norm(x, g, eps=1e-6):
    xf = x.astype(jnp.float32)
    y = xf * lax.rsqrt(jnp.mean(xf * xf, axis=-1, keepdims=True) + eps)
    return (y * g.astype(jnp.float32)).astype(x.dtype)

def partial_rope(x, pos):
    half = ROPE_DIM // 2
    inv = jnp.power(ROPE_THETA, -jnp.arange(half, dtype=jnp.float32) * 2.0 / ROPE_DIM)
    ang = pos.astype(jnp.float32)[:, None] * inv[None, :]
    cos = jnp.cos(ang)[None, :, None, :]
    sin = jnp.sin(ang)[None, :, None, :]
    xf = x.astype(jnp.float32)
    x1, x2, rest = xf[..., :half], xf[..., half:ROPE_DIM], xf[..., ROPE_DIM:]
    out = jnp.concatenate([x1 * cos - x2 * sin, x2 * cos + x1 * sin, rest], axis=-1)
    return out.astype(x.dtype)

def dsa_attention(q, k, v, iq, iw, ik, k_top):
    bsz, n_pad, n_heads, d_head = q.shape
    n_blocks = n_pad // BLOCK
    key_idx = jnp.arange(n_pad)
    gather = jax.vmap(lambda arr, idx: arr[idx])

    def one_block(i):
        t0 = i * BLOCK
        qb = lax.dynamic_slice_in_dim(q, t0, BLOCK, axis=1)
        iqb = lax.dynamic_slice_in_dim(iq, t0, BLOCK, axis=1)
        iwb = lax.dynamic_slice_in_dim(iw, t0, BLOCK, axis=1).astype(jnp.float32) * IDX_HEADS ** -0.5
        q_idx = t0 + jnp.arange(BLOCK)
        admissible = (key_idx[None, :] <= q_idx[:, None]) & (key_idx[None, :] >= PAD)
        dots = jnp.einsum('bqhd,bkd->bqhk', iqb, ik).astype(jnp.float32) * IDX_DIM ** -0.5
        score = jnp.einsum('bqh,bqhk->bqk', iwb, jax.nn.relu(dots))
        score = jnp.where(admissible[None], score, NEG)
        _, sel = lax.top_k(score, k_top)
        valid = (sel <= q_idx[None, :, None]) & (sel >= PAD)
        k_sel = gather(k, sel)
        v_sel = gather(v, sel)
        logits = jnp.einsum('bqhd,bqkd->bqhk', qb, k_sel).astype(jnp.float32) * d_head ** -0.5
        logits = jnp.where(valid[:, :, None, :], logits, NEG)
        probs = jax.nn.softmax(logits, axis=-1).astype(v.dtype)
        return jnp.einsum('bqhk,bqkd->bqhd', probs, v_sel)

    out = lax.map(one_block, jnp.arange(n_blocks))
    return jnp.moveaxis(out, 0, 1).reshape(bsz, n_pad, n_heads, d_head)

def forgetting_attention(q, k, v, log_f):
    bsz, n_pad, n_heads, d_head = q.shape
    n_blocks = n_pad // BLOCK
    key_idx = jnp.arange(n_pad)
    c = jnp.moveaxis(jnp.cumsum(log_f, axis=1), 1, 2)

    def one_block(i):
        t0 = i * BLOCK
        qb = lax.dynamic_slice_in_dim(q, t0, BLOCK, axis=1)
        cq = lax.dynamic_slice_in_dim(c, t0, BLOCK, axis=2)
        q_idx = t0 + jnp.arange(BLOCK)
        mask = (key_idx[None, :] <= q_idx[:, None]) & (key_idx[None, :] >= PAD)
        logits = (jnp.einsum('bqhd,bkhd->bhqk', qb, k).astype(jnp.float32) * d_head ** -0.5
                  + cq[..., None] - c[:, :, None, :])
        logits = jnp.where(mask[None, None], logits, NEG)
        probs = jax.nn.softmax(logits, axis=-1).astype(v.dtype)
        return jnp.einsum('bhqk,bkhd->bqhd', probs, v)

    out = lax.map(one_block, jnp.arange(n_blocks))
    return jnp.moveaxis(out, 0, 1).reshape(bsz, n_pad, n_heads, d_head)

def gla_chunked(q, k, v, log_a):
    bsz, n_pad, n_heads, d_k = q.shape
    d_v = v.shape[-1]
    n_chunks = n_pad // GLA_CHUNK

    def to_chunks(a):
        return jnp.moveaxis(a.reshape(bsz, n_chunks, GLA_CHUNK, *a.shape[2:]), 1, 0)

    causal = jnp.tril(jnp.ones((GLA_CHUNK, GLA_CHUNK), dtype=bool))

    def step(state, inp):
        qc, kc, vc, gc = inp
        b = jnp.cumsum(gc, axis=1)
        o_inter = jnp.einsum('bthd,bhde->bthe', qc * jnp.exp(b), state)
        diff = b[:, :, None] - b[:, None, :]
        decay = jnp.where(causal[None, :, :, None, None], jnp.exp(jnp.minimum(diff, 0.0)), 0.0)
        att = jnp.einsum('bthd,bshd,btshd->bhts', qc, kc, decay)
        o_intra = jnp.einsum('bhts,bshe->bthe', att, vc)
        b_last = b[:, -1]
        state = (state * jnp.exp(b_last)[..., None]
                 + jnp.einsum('bshd,bshe->bhde', kc * jnp.exp(b_last[:, None] - b), vc))
        return state, o_inter + o_intra

    s0 = jnp.zeros((bsz, n_heads, d_k, d_v), jnp.float32)
    _, out = lax.scan(step, s0, (to_chunks(q), to_chunks(k), to_chunks(v), to_chunks(log_a)))
    return jnp.moveaxis(out, 0, 1).reshape(bsz, n_pad, n_heads, d_v)

def hybrid_layer(h, pos, k_top, attn_norm, w_in, dsa_q_norm, dsa_k_norm, fox_q_norm, fox_k_norm,
                 fox_f_bias, gla_gate_w2, gla_gate_b, gla_out_norm, w_out, ffn_norm, w_gate_up, w_down):
    bsz, n_tok, _ = h.shape
    n_pad = n_tok + PAD
    a = rms_norm(h, attn_norm)
    proj = jnp.pad(a @ w_in, ((0, 0), (PAD, 0), (0, 0)))
    split_points = np.cumsum(IN_SPLITS)[:-1].tolist()
    (dq, dk, dv, iq, iw, ik, fq, fk, fv, ff, gq, gk, gv, gg, glr) = jnp.split(proj, split_points, axis=-1)

    def heads(t, n):
        return t.reshape(bsz, n_pad, n, t.shape[-1] // n)

    dq = partial_rope(rms_norm(heads(dq, DSA_HEADS), dsa_q_norm), pos)
    dk = partial_rope(rms_norm(dk, dsa_k_norm)[:, :, None], pos)[:, :, 0]
    iq = partial_rope(heads(iq, IDX_HEADS), pos)
    ik = partial_rope(ik[:, :, None], pos)[:, :, 0]
    o_a = dsa_attention(dq, dk, dv, iq, iw, ik, k_top)

    fq = rms_norm(heads(fq, FOX_HEADS), fox_q_norm)
    fk = rms_norm(heads(fk, FOX_HEADS), fox_k_norm)
    log_f = jax.nn.log_sigmoid((ff + fox_f_bias).astype(jnp.float32))
    o_b = forgetting_attention(fq, fk, heads(fv, FOX_HEADS), log_f)

    log_a = jax.nn.log_sigmoid((glr @ gla_gate_w2 + gla_gate_b).astype(jnp.float32)) / GLA_TAU
    o_c = gla_chunked(heads(gq, GLA_HEADS).astype(jnp.float32) * GLA_DK ** -0.5,
                      heads(gk, GLA_HEADS).astype(jnp.float32),
                      heads(gv, GLA_HEADS).astype(jnp.float32),
                      heads(log_a, GLA_HEADS))
    o_c = rms_norm(o_c, gla_out_norm).astype(h.dtype) * jax.nn.silu(heads(gg, GLA_HEADS))

    mixed = jnp.concatenate([o_a.reshape(bsz, n_pad, -1), o_b.reshape(bsz, n_pad, -1),
                             o_c.reshape(bsz, n_pad, -1)], axis=-1)[:, PAD:]
    h = h + mixed @ w_out

    f = rms_norm(h, ffn_norm)
    gate, up = jnp.split(f @ w_gate_up, 2, axis=-1)
    return h + (jax.nn.silu(gate) * up) @ w_down

def setup_inputs(seed: int = 0) -> dict:
    key = jax.random.key(seed)
    ks = jax.random.split(key, 16)
    f32 = jnp.float32

    def normal(k, shape, scale):
        return jax.random.normal(k, shape, f32) * scale

    def gain(k, shape):
        return 1.0 + 0.02 * jax.random.normal(k, shape, f32)

    return {
        'x': normal(ks[0], (BATCH, SEQ, D_MODEL), 1.0),
        'meta_tokens': normal(ks[1], (N_META, D_MODEL), 1.0),
        'attn_norm': gain(ks[2], (DEPTH, D_MODEL)),
        'w_in': normal(ks[3], (DEPTH, D_MODEL, N_IN), D_MODEL ** -0.5),
        'dsa_q_norm': gain(ks[4], (DEPTH, HEAD_DIM)),
        'dsa_k_norm': gain(ks[5], (DEPTH, HEAD_DIM)),
        'fox_q_norm': gain(ks[6], (DEPTH, HEAD_DIM)),
        'fox_k_norm': gain(ks[7], (DEPTH, HEAD_DIM)),
        'fox_f_bias': 2.0 + normal(ks[8], (DEPTH, FOX_HEADS), 0.1),
        'gla_gate_w2': normal(ks[9], (DEPTH, GLA_RANK, GLA_HEADS * GLA_DK), GLA_RANK ** -0.5),
        'gla_gate_b': normal(ks[10], (DEPTH, GLA_HEADS * GLA_DK), 0.1),
        'gla_out_norm': gain(ks[11], (DEPTH, GLA_DV)),
        'w_out': normal(ks[12], (DEPTH, D_MIX, D_MODEL), D_MIX ** -0.5),
        'ffn_norm': gain(ks[13], (DEPTH, D_MODEL)),
        'w_gate_up': normal(ks[14], (DEPTH, D_MODEL, 2 * D_FF), D_MODEL ** -0.5),
        'w_down': normal(ks[15], (DEPTH, D_FF, D_MODEL), D_FF ** -0.5),
    }

def reference(x, meta_tokens, attn_norm, w_in, dsa_q_norm, dsa_k_norm, fox_q_norm, fox_k_norm,
              fox_f_bias, gla_gate_w2, gla_gate_b, gla_out_norm, w_out, ffn_norm, w_gate_up, w_down):
    bsz, seq, _ = x.shape
    k_top = min(TOPK_MAX, seq // 4)
    meta = jnp.broadcast_to(meta_tokens[None].astype(x.dtype), (bsz, N_META, D_MODEL))
    h = jnp.concatenate([meta, x], axis=1)
    pos = jnp.arange(PAD + N_META + seq) - PAD
    for l in range(DEPTH):
        h = hybrid_layer(h, pos, k_top, attn_norm[l], w_in[l], dsa_q_norm[l], dsa_k_norm[l],
                         fox_q_norm[l], fox_k_norm[l], fox_f_bias[l], gla_gate_w2[l], gla_gate_b[l],
                         gla_out_norm[l], w_out[l], ffn_norm[l], w_gate_up[l], w_down[l])
    return h[:, N_META:]


_drawn_inputs = setup_inputs


def setup_inputs(seed=0):
    import zlib

    import numpy as np

    out = dict(_drawn_inputs(seed))
    spreads = {}
    factors = {'dsa_q_norm': 8.0,
     'dsa_k_norm': 8.0,
     'fox_q_norm': 8.0,
     'fox_k_norm': 8.0,
     'gla_out_norm': 4.125}
    for name, (base, spread) in spreads.items():
        noise = np.random.default_rng([zlib.crc32(name.encode()), seed]).standard_normal(out[name].shape)
        drawn = base * np.exp(spread * noise) if base else spread * noise
        out[name] = jnp.asarray(drawn.astype(out[name].dtype))
    for name, factor in factors.items():
        out[name] = (out[name] * factor).astype(out[name].dtype)
    return out
```

```python
from contextlib import ExitStack

import numpy as np
import concourse.bass as bass
from concourse import mybir

F32 = mybir.dt.float32
F32R = mybir.dt.float32r
BF16 = mybir.dt.bfloat16
I32 = mybir.dt.int32
ALU = mybir.AluOpType
ACT = mybir.ActivationFunctionType
AX = mybir.AxisListType

DEPTH, D, SEQ, META = 2, 1024, 512, 16
N = META + SEQ
HALF, BLK = N // 2, 88
NB = N // BLK
KT = D // 128
FF = 2816
MF = FF // 128
TOPK = 128
EPS = 1e-6
NEG, TAKEN = -1e30, -3e38
RANK = 16
TAU = 16.0

DQ, DKIK, IQ, SMALL, FQ, FK, FV, GQ, GK, GV, GG = 0, 2, 3, 5, 6, 8, 10, 12, 14, 16, 20
N_PROJ, N_OUT, N_GU, N_DN = 24, KT, 2 * MF, 3 * KT
UNITS = N_PROJ + N_OUT + N_GU + N_DN
U_OUT, U_GU, U_DN = N_PROJ, N_PROJ + N_OUT, N_PROJ + N_OUT + N_GU
DN_PARTS = (8, 8, 6)
ROW_DV, ROW_LR, ROW_FF, ROW_IW = 0, 64, 96, 100

P_ATT, P_FFN, P_DQ, P_DK, P_FQ, P_FK, P_GO, P_GB, P_FB, P_W2 = 0, 8, 16, 17, 18, 19, 20, 21, 23, 24
N_PAR = P_W2 + 256
C_ID, C_ONE, C_BLK, C_ROT, C_COS, C_SIN = 0, 128, 256, 384, 512, 512 + N
C_RST = C_SIN + N
C_CAU = C_RST + N
C_TRI = C_CAU + BLK
C_SEL = C_TRI + BLK
C_EPS = C_SEL + 4 * BLK
N_CST = C_EPS + 1

TOPK_ROUNDS = 2
CHOOSE_TOTAL = (NB - 1) * (4 + TOPK // 8 // TOPK_ROUNDS + 1)
ATTEND_PER_HALF = 5

NORMED = {0: P_DQ, 1: P_DQ, 2: P_DK, 6: P_FQ, 7: P_FQ, 8: P_FK, 9: P_FK}
ROPED = (0, 1, 2, 3, 4)


def attention_steps(groups):
    heads = [(g, i, h) for g, i in groups for h in range(4)]
    steps = []
    for n in range(len(heads) + 2):
        if n < len(heads):
            steps.append(("logits", *heads[n]))
        if 1 <= n <= len(heads):
            steps.append(("turn", *heads[n - 1]))
        if n >= 2:
            g, i, h = heads[n - 2]
            steps.append(("values", g, i, h))
            if h == 3:
                steps += [("heads", g, i), ("mixed", g, i)]
    return steps


def plan():
    steps = []
    for k in range(6):
        steps += [("proj", k, 0), ("proj", k, 1)]
        if k in (0, 1, 2):
            steps += [("square", k)]
        if k in (1, 2, 3):
            steps += [("norm", k - 1)]
        if k >= 3:
            steps += [("rope", (2, 0, 1)[k - 3])] + ([("copies",)] if k == 3 else [])
    steps += [("rope", 3), ("rope", 4), ("turn_tile", SMALL), ("gate", 0), ("gate", 1), ("gates",)]

    choose = []
    for i in range(1, NB):
        choose += [("index", i, h) for h in range(4)]
        choose += [("topk", i, r) for r in range(0, TOPK // 8, TOPK_ROUNDS)] + [("select", i)]
    attend = attention_steps([(0, 0), (0, 1), (1, 0), (1, 1), (0, 2), (1, 2), (0, 3), (1, 3), (0, 4), (1, 4), (1, 5), (0, 5)])

    after = {k: [] for k in range(6, N_PROJ)}
    for k in (6, 7, 8, 9):
        after[k] += [("square", k)]
        after[k + 1] += [("norm", k)]
    after[11] += [("turn_tile", FV)]
    after[12] += [("turn_tile", FV + 1)]
    after[15] += [("decays",)]
    after[16] += [("turn_k", 0), ("turn_k", 1)]
    for k in range(GV, GV + 4):
        after[k + 1] += [("turn_tile", k)]
    for c in range(3):
        after[GG + 1 + c] += [("gla_att", c), ("gla_out", c), ("gla_kv", c)]

    def may_start(step):
        if step[0] != "logits":
            return True
        g, i = step[1:3]
        return ("turn_tile", FV + 1) in steps if g else (i == 0 or ("select", i) in steps)

    halves = 2 * (N_PROJ - 6)
    n = 0
    for k in range(6, N_PROJ):
        for hf in range(2):
            steps.append(("proj", k, hf))
            if hf == 1:
                steps += after[k]
            n += 1
            while choose and len(choose) > CHOOSE_TOTAL * (1 - n / halves):
                steps.append(choose.pop(0))
            for _ in range(ATTEND_PER_HALF):
                if attend and may_start(attend[0]):
                    steps.append(attend.pop(0))
    tail = []
    for c in range(3, NB):
        tail += [("gla_att", c), ("gla_out", c)] + ([("gla_kv", c)] if c < NB - 1 else [])
    for h in range(4):
        tail += [("square", GV + h), ("silu", h), ("norm", GV + h), ("gla_mix", h)]
    while tail or attend:
        for q, count in ((attend, 3), (tail, 1)):
            for _ in range(count):
                if q:
                    steps.append(q.pop(0))
    return steps


STEPS = plan()
AUX_KINDS = ("norm", "rope", "turn_tile", "gate", "index", "logits", "turn", "turn_k", "gla_att", "gla_out", "gla_kv")
AUX = {s: n + 1 for n, s in enumerate([s for s in STEPS if s[0] in AUX_KINDS])}
AUX[("prenorm", 0)] = 0
AUX[("prenorm", 1)] = len(AUX)
SQUARES = {s[1]: n for n, s in enumerate([s for s in STEPS if s[0] == "square"])}
LOGITS = {s[1:]: n for n, s in enumerate([s for s in STEPS if s[0] == "logits"])}
GROUPS = {s[1:]: n for n, s in enumerate([s for s in STEPS if s[0] == "heads"])}
ROPES = {s[1]: n for n, s in enumerate([s for s in STEPS if s[0] == "rope"])}
NORMS = {s[1]: n for n, s in enumerate([s for s in STEPS if s[0] == "norm"])}
INDEX = {s[1:]: n for n, s in enumerate([s for s in STEPS if s[0] == "index"])}


def turn_of(job):
    n = AUX[job]
    return n % 2, n // 2 + 1


def hybrid_block(nc, hT, weights, params, consts, out):
    with ExitStack() as ctx:
        def sb(name, shape, dt=F32, scope=ctx):
            return scope.enter_context(nc.sbuf_tensor(name, shape, dt))

        def sem(name):
            return ctx.enter_context(nc.semaphore(name))

        h = sb("h", [128, KT, N])
        xhi = sb("xhi", [128, KT, N], F32R)
        xlo = sb("xlo", [128, KT, N], F32R)
        raw = sb("raw", [128, 2, KT, 128])
        whi = sb("whi", [128, 2, KT, 128], F32R)
        wlo = sb("wlo", [128, 2, KT, 128], F32R)
        cst = sb("cst", [128, N_CST])
        par_all = sb("par_all", [128, DEPTH, N_PAR])
        par = sb("par", [128, N_PAR])
        sqb = sb("sqb", [128, 2, N])
        rnb = sb("rnb", [128, 2, N])
        xnb = sb("xnb", [128, 2, N])
        with ExitStack() as mixers:
            def mb(name, shape, dt=F32):
                return sb(name, shape, dt, mixers)
            feat = mb("feat", [128, N_PROJ, N])
            kk = mb("kk", [128, 2, N])
            tok_small = mb("tok_small", [BLK, NB, 128])
            v_fox = mb("v_fox", [BLK, NB, 256])
            v_gla = mb("v_gla", [BLK, NB, 512])
            k_gla = mb("k_gla", [BLK, NB, 256])
            relu = mb("relu", [BLK, 2, N])
            score = mb("score", [BLK, N])
            top8 = mb("top8", [BLK, 8])
            selb = mb("selb", [BLK, 2, N], BF16)
            ident16 = mb("ident16", [BLK, BLK], BF16)
            causal16 = mb("causal16", [BLK, BLK], BF16)
            probs = mb("probs", [BLK, 2, N])
            probs_t = mb("probs_t", [BLK, 2, NB, BLK])
            stat = mb("stat", [BLK, 4, 48])
            o_tok = mb("o_tok", [BLK, 256])
            fox_c = mb("fox_c", [128, N])
            att = mb("att", [BLK, 2, 2, BLK])
            state = mb("state", [128, 2, 128])
            coef = mb("coef", [128, 2, NB])
        with ExitStack() as ffn:
            hhi = sb("hhi", [128, MF, N], F32R, ffn)
            hlo = sb("hlo", [128, MF, N], F32R, ffn)
            sg = sb("sg", [128, 2, N], F32, ffn)
            hid = sb("hid", [128, 2, N], F32, ffn)
        ps = ctx.enter_context(nc.psum_tensor("ps", [128, 8 * 512], F32))

        loaded = sem("loaded")
        raw_loaded = [sem("raw_loaded0"), sem("raw_loaded1")]
        hi_done = sem("hi_done")
        split_done = sem("split_done")
        half_done = sem("half_done")
        layer_open = sem("layer_open")
        stored = sem("stored")
        par_ready = sem("par_ready")
        engines_done = sem("engines_done")
        sq_ready = sem("sq_ready")
        ssq_taken = sem("ssq_taken")
        rstd_ready = sem("rstd_ready")
        xn_ready = sem("xn_ready")
        xhi_ready = sem("xhi_ready")
        x_ready = sem("x_ready")
        feat_ready = sem("feat_ready")
        job_done = [sem("job_done0"), sem("job_done1")]
        job_taken = [sem("job_taken0"), sem("job_taken1")]
        normed = sem("normed")
        roped = sem("roped")
        copied = sem("copied")
        gate_step = sem("gate_step")
        gate_ln = sem("gate_ln")
        decay_arg = sem("decay_arg")
        decay_exp = sem("decay_exp")
        decayed = sem("decayed")
        fox_ready = sem("fox_ready")
        index_used = sem("index_used")
        selected = sem("selected")
        max_ready = sem("max_ready")
        values_done = sem("values_done")
        heads_ready = sem("heads_ready")
        heads_turned = sem("heads_turned")
        mixed_ready = sem("mixed_ready")
        state_ready = sem("state_ready")
        silu_exp = sem("silu_exp")
        gla_mixed = sem("gla_mixed")
        rn_ready = sem("rn_ready")
        acc_free = sem("acc_free")
        sg_ready = sem("sg_ready")
        hhi_ready = sem("hhi_ready")
        hid_ready = sem("hid_ready")
        act_step = sem("act_step")
        dve_step = sem("dve_step")
        layer_sems = range(par_ready.num, dve_step.num + 1)

        def cols(base, n, rows=slice(0, 128)):
            return cst[rows, base:base + n]

        def bank(b, n, rows=slice(0, 128)):
            return ps[rows, b * 512:b * 512 + n]

        def two_banks(b):
            return ps[:, b * 512:(b + 2) * 512].rearrange("p (a c) -> p a c", a=2)[:, :, 0:HALF]

        def halves(ap):
            return ap.rearrange("p (a c) -> p a c", a=2)

        def block_of(i):
            return slice(i * BLK, (i + 1) * BLK)

        def head_rows(hd):
            return slice(64 * (hd % 2), 64 * (hd % 2) + 64)

        def mix_tile(m):
            return feat[:, (0, 1, 6, 7, 20, 21, 22, 23)[m], :]

        block = ctx.enter_context(nc.Block())

        @block.sync
        def _(sp):
            with sp.Fori(0, DEPTH) as l:
                with sp.Fori(0, UNITS // 2) as j:
                    for b in range(2):
                        sp.wait_ge(split_done, l * UNITS + j * 2 + (b + 1))
                        sp.dma_start(raw[:, b].rearrange("p k n -> p (k n)"),
                                     weights[l, j * 2 + b]).then_inc(raw_loaded[b], 16)
            sp.wait_ge(layer_open, DEPTH)
            sp.dma_start(out.rearrange("(k p) t -> p k t", p=128), h[:, :, META:N]).then_inc(stored, 16)
            sp.wait_ge(stored, 16)

        @block.gpsimd
        def _(pool):
            pool.sem_inc(split_done, 2)
            with pool.Fori(0, DEPTH) as l:
                with pool.Fori(0, UNITS // 2) as j:
                    for b in range(2):
                        unit = l * UNITS + j * 2 + b
                        pool.wait_ge(raw_loaded[b], (l * (UNITS // 2) + j + 1) * 16)
                        pool.wait_ge(half_done, unit * 2 + 2)
                        pool.sem_inc(hi_done, 1)
                        nc.gpsimd.tensor_copy(whi[:, b], raw[:, b]).then_inc(hi_done, 1)
                        pool.wait_ge(hi_done, unit * 2 + 2)
                        nc.gpsimd.tensor_tensor(wlo[:, b], raw[:, b], whi[:, b].bitcast(F32),
                                                ALU.subtract).then_inc(split_done, 1)

        @block.tensor
        def _(pe):
            pe.sem_inc(half_done, 4)
            pe.wait_ge(loaded, 48)
            with pe.Fori(0, DEPTH) as l:
                unit0 = pe.snap(l * UNITS + 2)
                ident, ones = cols(C_ID, 128), cols(C_ONE, 128)
                pe.wait_ge(par_ready, 4)

                def job_begin(job):
                    p, n = turn_of(job)
                    if n > 1:
                        pe.wait_ge(job_taken[p], n - 1)
                    return 4 + 2 * p, job_done[p]

                def wait_taken(job):
                    p, n = turn_of(job)
                    pe.wait_ge(job_taken[p], n)

                def unit_half(b, bank_no, hf, kts, first, last, src_hi, src_lo, k0=0, wait=None):
                    for k in range(kts):
                        if wait is not None:
                            pe.wait_ge(wait, k + 1)
                        for t, (w, x) in enumerate(((whi, src_hi), (whi, src_lo), (wlo, src_hi))):
                            ins = nc.tensor.matmul(bank(bank_no, HALF), w[:, b, k],
                                                   x[:, k0 + k, hf * HALF:(hf + 1) * HALF],
                                                   start=(first and k == 0 and t == 0),
                                                   stop=(last and k == kts - 1 and t == 2))
                    ins.then_inc(half_done, 1)

                def prenorm(s):
                    b0, done = job_begin(("prenorm", s))
                    for k in range(KT):
                        pe.wait_ge(sq_ready, k + 1 if s == 0 else len(SQUARES) + KT + k + 1)
                        for hf in range(2):
                            ins = nc.tensor.matmul(bank(b0 + hf, HALF), ones, sqb[:, k % 2, hf * HALF:(hf + 1) * HALF],
                                                   start=(k == 0), stop=(k == KT - 1))
                        if k < KT - 1:
                            ins.then_inc(ssq_taken, 1)
                    ins.then_inc(done, 1)

                def proj(k, hf):
                    q = 2 * k + hf
                    if hf == 0:
                        pe.wait_ge(split_done, unit0 + (k + 1))
                    if q >= 3:
                        pe.wait_ge(feat_ready, q - 2)
                    unit_half(k % 2, q % 3, hf, KT, True, True, xhi, xlo, wait=x_ready if q == 0 else None)

                def norm(k):
                    b0, done = job_begin(("norm", k))
                    pe.wait_ge(sq_ready, KT + SQUARES[k] + 1)
                    lhs = cols(C_BLK, 128) if k < GV else ones
                    for hf in range(2):
                        ins = nc.tensor.matmul(bank(b0 + hf, HALF), lhs,
                                               sqb[:, SQUARES[k] % 2, hf * HALF:(hf + 1) * HALF], start=True, stop=True)
                    ins.then_inc(done, 1)

                def rope(k):
                    b0, done = job_begin(("rope", k))
                    if k in NORMS:
                        pe.wait_ge(normed, NORMS[k] + 1)
                    pe.wait_ge(feat_ready, 2 * k + 2)
                    for hf in range(2):
                        ins = nc.tensor.matmul(bank(b0 + hf, HALF), cols(C_ROT, 128),
                                               feat[:, k, hf * HALF:(hf + 1) * HALF], start=True, stop=True)
                    ins.then_inc(done, 1)

                def turn_tile(k):
                    b0, done = job_begin(("turn_tile", k))
                    pe.wait_ge(feat_ready, 2 * k + 2)
                    turn_blocks(feat[:, k, :], b0, done)

                def turn_k(t):
                    b0, done = job_begin(("turn_k", t))
                    pe.wait_ge(decayed, 2)
                    turn_blocks(feat[:, GK + t, :], b0, done)

                def turn_blocks(src, b0, done):
                    for i in range(NB):
                        col = (b0 + i // 3) * 512 + (i % 3) * 128
                        ins = nc.tensor.transpose(ps[0:BLK, col:col + 128], src[:, block_of(i)], ident)
                    ins.then_inc(done, 1)

                def gate(t):
                    b0, done = job_begin(("gate", t))
                    pe.wait_ge(feat_ready, 2 * SMALL + 2)
                    rows = slice(ROW_LR, ROW_LR + RANK)
                    for hf in range(2):
                        ins = nc.tensor.matmul(bank(b0 + hf, HALF), par[rows, P_W2 + t * 128:P_W2 + (t + 1) * 128],
                                               feat[rows, SMALL, hf * HALF:(hf + 1) * HALF], start=True, stop=True)
                    ins.then_inc(done, 1)

                def pieces(n):
                    return [(0, min(n, 512))] + ([(512, n)] if n > 512 else [])

                def index(i, hd):
                    b0, done = job_begin(("index", i, hd))
                    if (i, hd) == (1, 0):
                        pe.wait_ge(roped, len(ROPES))
                        pe.wait_ge(copied, 2)
                    r = head_rows(hd)
                    for a, z in pieces((i + 1) * BLK):
                        ins = nc.tensor.matmul(ps[0:BLK, b0 * 512 + a:b0 * 512 + z], feat[r, IQ + hd // 2, block_of(i)],
                                               kk[r, 1, a:z], start=True, stop=True)
                    ins.then_inc(done, 1)

                def logits(g, i, hd):
                    b0, done = job_begin(("logits", g, i, hd))
                    r = head_rows(hd)
                    n = (i + 1) * BLK
                    if g == 0:
                        q, key = feat[r, DQ + hd // 2, block_of(i)], kk[r, 0, :]
                        if hd == 0:
                            pe.wait_ge(roped, len(ROPES))
                            pe.wait_ge(copied, 2)
                            if i:
                                pe.wait_ge(selected, i)
                    else:
                        q, key = feat[r, FQ + hd // 2, block_of(i)], feat[r, FK + hd // 2, :]
                        if hd == 0:
                            pe.wait_ge(normed, NORMS[FK + 1] + 1)
                            pe.wait_ge(fox_ready, 1)
                    for a, z in pieces(n):
                        o = ps[0:BLK, b0 * 512 + a:b0 * 512 + z]
                        last = z == n and g == 0 and i > 0
                        ins = nc.tensor.matmul(o, q, key[:, a:z], start=True, stop=False)
                        if g == 1:
                            rows = slice(ROW_FF, ROW_FF + 4)
                            ins = nc.tensor.matmul(o, cst[rows, C_SEL + hd * BLK:C_SEL + (hd + 1) * BLK],
                                                   fox_c[rows, a:z], start=False, stop=(z <= i * BLK))
                        if g == 0 and i > 0:
                            ins = nc.tensor.matmul(o, ident16[:], selb[:, i % 2, a:z], start=False, stop=True)
                        else:
                            lo = max(a, i * BLK)
                            if z > lo:
                                ins = nc.tensor.matmul(ps[0:BLK, b0 * 512 + lo:b0 * 512 + z], ident16[:],
                                                       causal16[:, lo - i * BLK:z - i * BLK], start=False, stop=True)
                    ins.then_inc(done, 1)

                def turn(g, i, hd):
                    b0, done = job_begin(("turn", g, i, hd))
                    wait_taken(("logits", g, i, hd))
                    u = LOGITS[(g, i, hd)]
                    for j in range(i + 1):
                        col = b0 * 512 + (j * BLK if i < NB - 1 else (j // 3) * 512 + (j % 3) * BLK)
                        ins = nc.tensor.transpose(ps[0:BLK, col:col + BLK], probs[:, u % 2, block_of(j)],
                                                  cols(C_ID, BLK, slice(0, BLK)))
                    ins.then_inc(done, 1)

                def values(g, i, hd):
                    wait_taken(("turn", g, i, hd))
                    u, grp = LOGITS[(g, i, hd)], GROUPS[(g, i)]
                    if hd == 0:
                        if grp:
                            pe.wait_ge(mixed_ready, grp)
                        for t in ((SMALL,) if g == 0 else (FV, FV + 1)):
                            wait_taken(("turn_tile", t))
                    for j in range(i + 1):
                        v = tok_small[:, j, 0:64] if g == 0 else v_fox[:, j, hd * 64:(hd + 1) * 64]
                        ins = nc.tensor.matmul(ps[0:BLK, 3 * 512 + hd * 64:3 * 512 + (hd + 1) * 64],
                                               probs_t[:, u % 2, j, :], v, start=(j == 0), stop=(j == i))
                    ins.then_inc(values_done, 1)

                def heads(g, i):
                    grp = GROUPS[(g, i)]
                    pe.wait_ge(heads_ready, grp + 1)
                    for t in range(2):
                        ins = nc.tensor.transpose(ps[:, 3 * 512 + t * BLK:3 * 512 + (t + 1) * BLK],
                                                  o_tok[:, t * 128:(t + 1) * 128], cols(C_ID, BLK, slice(0, BLK)))
                    ins.then_inc(heads_turned, 1)

                def gla_place(b0, hd):
                    col = (b0 + hd % 2) * 512 + (hd // 2) * BLK
                    return ps[:, col:col + BLK]

                def gla_att(c):
                    b0, done = job_begin(("gla_att", c))
                    pe.wait_ge(decayed, 2)
                    for hd in range(4):
                        r = head_rows(hd)
                        ins = nc.tensor.matmul(gla_place(b0, hd)[0:BLK],
                                               feat[r, GK + hd // 2, block_of(c)], feat[r, GQ + hd // 2, block_of(c)],
                                               start=True, stop=True)
                    ins.then_inc(done, 1)

                def gla_out(c):
                    b0, done = job_begin(("gla_out", c))
                    wait_taken(("gla_att", c))
                    if c == 0:
                        for t in range(4):
                            wait_taken(("turn_tile", GV + t))
                    else:
                        pe.wait_ge(state_ready, c)
                    for hd in range(4):
                        r = head_rows(hd)
                        o = gla_place(b0, hd)
                        if c:
                            nc.tensor.matmul(o, state[r, hd // 2, :], feat[r, GQ + hd // 2, block_of(c)],
                                             start=True, stop=False)
                        ins = nc.tensor.matmul(o, v_gla[:, c, hd * 128:(hd + 1) * 128], att[:, hd % 2, hd // 2, :],
                                               start=(c == 0), stop=True)
                    ins.then_inc(done, 1)

                def gla_kv(c):
                    b0, done = job_begin(("gla_kv", c))
                    if c == 0:
                        for t in range(2):
                            wait_taken(("turn_k", t))
                    for t in range(2):
                        ins = nc.tensor.matmul(ps[:, b0 * 512 + t * 256:b0 * 512 + (t + 1) * 256],
                                               k_gla[:, c, t * 128:(t + 1) * 128], v_gla[:, c, t * 256:(t + 1) * 256],
                                               start=True, stop=True)
                    ins.then_inc(done, 1)

                do = dict(proj=proj, norm=norm, rope=rope, turn_tile=turn_tile, turn_k=turn_k, gate=gate, index=index,
                          logits=logits, turn=turn, values=values, heads=heads, gla_att=gla_att, gla_out=gla_out,
                          gla_kv=gla_kv)
                prenorm(0)
                for step in STEPS:
                    if step[0] in do:
                        do[step[0]](*step[1:])

                pe.wait_ge(x_ready, 2 * KT)
                pe.wait_ge(acc_free, 2)
                pe.wait_ge(feat_ready, 2 * N_PROJ)
                pe.wait_ge(mixed_ready, len(GROUPS))
                with pe.Fori(0, N_OUT // 2) as j:
                    for b in range(2):
                        pe.wait_ge(split_done, unit0 + j * 2 + (U_OUT + b + 1))
                        pe.wait_ge(acc_free, j * 2 + (b + 1))
                        for hf in range(2):
                            unit_half(b, 2 * b + hf, hf, KT, True, True, xhi, xlo)

                prenorm(1)
                pe.wait_ge(acc_free, 2 + N_OUT)
                p, n = turn_of(("prenorm", 1))
                pe.wait_ge(job_taken[p], n)
                pe.wait_ge(job_taken[1 - p], (len(AUX) - n))
                pe.wait_ge(x_ready, 3 * KT)
                with pe.Fori(0, MF // 2) as j:
                    for b in range(2):
                        pe.wait_ge(acc_free, j * 2 + (N_OUT + b + 1))
                        for s in range(2):
                            pe.wait_ge(split_done, unit0 + j * 4 + (U_GU + 2 * b + s + 1))
                            for hf in range(2):
                                unit_half(s, 4 * b + 2 * s + hf, hf, KT, True, True, xhi, xlo)
                pe.wait_ge(hid_ready, MF)
                pe.wait_ge(acc_free, 2 + N_OUT + MF)
                with pe.Fori(0, KT // 2) as j:
                    for b in range(2):
                        pe.wait_ge(acc_free, j * 2 + (N_OUT + MF + b + 1))
                        for s, kts in enumerate(DN_PARTS):
                            pe.wait_ge(split_done, unit0 + j * 6 + (U_DN + 3 * b + s + 1))
                            for hf in range(2):
                                unit_half((3 * b + s) % 2, 2 * b + hf, hf, kts, s == 0, s == 2, hhi, hlo,
                                          k0=sum(DN_PARTS[:s]))
                pe.drain().then_inc(engines_done, 1)
                pe.wait_ge(layer_open, l + 1)

        @block.scalar
        def _(act):
            act.dma_start(h[:], hT.rearrange("(k p) t -> p k t", p=128)).then_inc(loaded, 16)
            act.dma_start(cst[:], consts).then_inc(loaded, 16)
            act.dma_start(par_all[:], params.rearrange("l p n -> p l n")).then_inc(loaded, 16)
            nc.scalar.preload_act_table_set("natural_log_exp_and_others")
            act.wait_ge(loaded, 48)
            eps = cols(C_EPS, 1)
            with act.Fori(0, DEPTH) as l:
                half0 = act.snap(l * (2 * UNITS) + 4)
                act.wait_ge(par_ready, 4)
                own = [0]

                def chain(ins):
                    own[0] += 1
                    ins.then_inc(act_step, 1)
                    act.wait_ge(act_step, own[0])

                def wait_done(job):
                    p, n = turn_of(job)
                    act.wait_ge(job_done[p], n)
                    return 4 + 2 * p, job_taken[p], n

                def rsqrt_mean(job, count, dst):
                    b0, taken, n = wait_done(job)
                    nc.scalar.activation(halves(dst), two_banks(b0), ACT.Ln, bias=eps, scale=1.0 / count).then_inc(taken, 1)
                    act.wait_ge(taken, n)

                def prenorm(s, gains):
                    for k in range(KT):
                        if k >= 2:
                            act.wait_ge(ssq_taken, s * (KT - 1) + k - 1)
                        nc.scalar.activation(sqb[:, k % 2], h[:, k], ACT.Square).then_inc(sq_ready, 1)
                    rsqrt_mean(("prenorm", s), D, rnb[:, 0])
                    nc.scalar.activation(rnb[:, 0], rnb[:, 0], ACT.Exp, scale=-0.5).then_inc(rstd_ready, 1)
                    for k in range(KT):
                        act.wait_ge(xn_ready, s * KT + k + 1)
                        nc.scalar.activation(xhi[:, k], xnb[:, k % 2], ACT.Copy,
                                             scale=par[:, gains + k:gains + k + 1]).then_inc(xhi_ready, 1)

                def proj(k, hf):
                    if k == GG and hf == 0:
                        act.wait_ge(decayed, 2)
                    act.wait_ge(half_done, half0 + (2 * k + hf + 1))
                    nc.scalar.activation(feat[:, k, hf * HALF:(hf + 1) * HALF], bank((2 * k + hf) % 3, HALF),
                                         ACT.Copy).then_inc(feat_ready, 1)

                def square(k):
                    n = SQUARES[k]
                    if k < GV:
                        act.wait_ge(feat_ready, 2 * k + 2)
                    else:
                        p, m = turn_of(("gla_out", NB - 1))
                        act.wait_ge(job_taken[p], m)
                    if n >= 2:
                        before = [s for s in STEPS if s[0] == "square"][n - 2][1]
                        wait_done(("norm", before))
                    else:
                        wait_done(("prenorm", 0))
                    nc.scalar.activation(sqb[:, n % 2], feat[:, k], ACT.Square).then_inc(sq_ready, 1)

                def norm(k):
                    n = NORMS[k]
                    if n >= 2:
                        act.wait_ge(normed, n - 1)
                    else:
                        act.wait_ge(xn_ready, KT)
                    dst = rnb[:, n % 2]
                    rsqrt_mean(("norm", k), 64 if k < GV else 128, dst)
                    nc.scalar.activation(dst, dst, ACT.Exp, scale=-0.5).then_inc(rn_ready, 1)

                def copies():
                    act.wait_ge(roped, ROPES[2] + 1)
                    nc.scalar.activation(kk[64:128, 0], kk[0:64, 0], ACT.Copy).then_inc(copied, 1)
                    nc.scalar.activation(kk[0:64, 1], kk[64:128, 1], ACT.Copy).then_inc(copied, 1)

                def take_blocks(job, dst):
                    b0, taken, _ = wait_done(job)
                    src = ps[0:BLK, b0 * 512:(b0 + 2) * 512].rearrange("p (a c) -> p a c", a=2)[:, :, 0:384]
                    nc.scalar.activation(dst.rearrange("p (a i) c -> p a i c", a=2),
                                         src.rearrange("p a (i c) -> p a i c", i=3), ACT.Copy).then_inc(taken, 1)

                def turn_tile(k):
                    take_blocks(("turn_tile", k),
                                tok_small[:] if k == SMALL else
                                v_fox[:, :, (k - FV) * 128:(k - FV + 1) * 128] if k < GV else
                                v_gla[:, :, (k - GV) * 128:(k - GV + 1) * 128])

                def turn_k(t):
                    take_blocks(("turn_k", t), k_gla[:, :, t * 128:(t + 1) * 128])

                def gate(t):
                    b0, taken, _ = wait_done(("gate", t))
                    nc.scalar.activation(halves(feat[:, GG + 2 + t]), two_banks(b0), ACT.Identity,
                                         bias=par[:, P_GB + t:P_GB + t + 1]).then_inc(taken, 1)

                def gates():
                    for t in range(2):
                        p, n = turn_of(("gate", t))
                        act.wait_ge(job_taken[p], n)
                    e = feat[:, GG:GG + 2]
                    chain(nc.scalar.activation(e, feat[:, GG + 2:GG + 4], ACT.Abs))
                    chain(nc.scalar.activation(e, e, ACT.Exp, scale=-1.0))
                    nc.scalar.activation(e, e, ACT.Ln, bias=cols(C_ONE, 1)).then_inc(gate_ln, 1)
                    rows = slice(ROW_FF, ROW_FF + 4)
                    act.wait_ge(feat_ready, 2 * SMALL + 2)
                    chain(nc.scalar.activation(fox_c[rows], feat[rows, SMALL], ACT.Identity,
                                               bias=par[rows, P_FB:P_FB + 1]))
                    act.wait_ge(roped, len(ROPES))
                    f = xnb[rows, 0]
                    chain(nc.scalar.activation(f, fox_c[rows], ACT.Abs))
                    chain(nc.scalar.activation(f, f, ACT.Exp, scale=-1.0))
                    nc.scalar.activation(f, f, ACT.Ln, bias=cols(C_ONE, 1, rows)).then_inc(gate_ln, 1)
                    act.wait_ge(decay_arg, 1)
                    nc.scalar.activation(coef[:, :, 0:NB - 1], coef[:, :, 0:NB - 1], ACT.Exp, scale=1.0 / TAU).then_inc(decay_exp, 1)
                    act.wait_ge(decay_arg, 2)
                    d = feat[:, GG + 2:GG + 4]
                    chain(nc.scalar.activation(e, d, ACT.Exp, scale=1.0 / TAU))
                    nc.scalar.activation(d, d, ACT.Exp, scale=-1.0 / TAU).then_inc(decay_exp, 1)

                def index(i, hd):
                    b0, taken, _ = wait_done(("index", i, hd))
                    n = INDEX[(i, hd)]
                    if n >= 2:
                        act.wait_ge(index_used, n - 1)
                    nk = (i + 1) * BLK
                    nc.scalar.activation(relu[:, n % 2, 0:nk], ps[0:BLK, b0 * 512:b0 * 512 + nk], ACT.Relu,
                                         scale=1.0 / 16).then_inc(taken, 1)

                def logits(g, i, hd):
                    b0, taken, _ = wait_done(("logits", g, i, hd))
                    u = LOGITS[(g, i, hd)]
                    act.wait_ge(max_ready, 2 * u + 2)
                    if u >= 2:
                        before = [s for s in STEPS if s[0] == "logits"][u - 2][1:]
                        wait_done(("turn",) + before)
                    nk = (i + 1) * BLK
                    nc.scalar.activation(probs[:, u % 2, 0:nk], ps[0:BLK, b0 * 512:b0 * 512 + nk], ACT.Exp,
                                         bias=stat[:, 1, u:u + 1], scale=0.125,
                                         accum_out=stat[:, 2, u:u + 1]).then_inc(taken, 1)

                def turn(g, i, hd):
                    b0, taken, _ = wait_done(("turn", g, i, hd))
                    u = LOGITS[(g, i, hd)]
                    if u >= 2:
                        act.wait_ge(values_done, u - 1)
                    if i < NB - 1:
                        nc.scalar.activation(probs_t[:, u % 2, 0:i + 1], ps[0:BLK, b0 * 512:b0 * 512 + (i + 1) * BLK]
                                             .rearrange("p (j q) -> p j q", q=BLK), ACT.Copy).then_inc(taken, 1)
                    else:
                        nc.scalar.activation(probs_t[:, u % 2].rearrange("p (a j) q -> p a (j q)", a=2),
                                             two_banks(b0)[0:BLK], ACT.Copy).then_inc(taken, 1)

                def gla_out(c):
                    b0, taken, _ = wait_done(("gla_out", c))
                    for a in range(2):
                        ins = nc.scalar.activation(feat[:, GV + a:GV + a + 3:2, block_of(c)], bank(b0 + a, 2 * BLK)
                                                   .rearrange("p (h t) -> p h t", h=2), ACT.Copy)
                    ins.then_inc(taken, 1)

                def silu(hd):
                    act.wait_ge(feat_ready, 2 * (GG + hd) + 2)
                    if hd >= 2:
                        act.wait_ge(gla_mixed, hd - 1)
                    else:
                        act.wait_ge(fox_ready, 1)
                        act.wait_ge(roped, len(ROPES))
                    nc.scalar.activation(xnb[:, hd % 2], feat[:, GG + hd], ACT.Exp, scale=-1.0).then_inc(silu_exp, 1)

                prenorm(0, P_ATT)
                do = dict(proj=proj, square=square, norm=norm, copies=copies, turn_tile=turn_tile, turn_k=turn_k,
                          gate=gate, gates=gates, index=index, logits=logits, turn=turn, gla_out=gla_out, silu=silu)
                for step in STEPS:
                    if step[0] in do:
                        do[step[0]](*step[1:])

                act.wait_ge(half_done, half0 + 2 * N_PROJ)
                act.wait_ge(mixed_ready, len(GROUPS))
                act.wait_ge(gla_mixed, 4)
                for m in range(KT):
                    nc.scalar.activation(xhi[:, m], mix_tile(m), ACT.Copy).then_inc(xhi_ready, 1)

                act.wait_ge(acc_free, 2 + N_OUT)
                prenorm2 = [0]
                for k in range(KT):
                    if k >= 2:
                        act.wait_ge(ssq_taken, (KT - 1) + k - 1)
                    nc.scalar.activation(sqb[:, k % 2], h[:, k], ACT.Square).then_inc(sq_ready, 1)
                rsqrt_mean(("prenorm", 1), D, rnb[:, 0])
                nc.scalar.activation(rnb[:, 0], rnb[:, 0], ACT.Exp, scale=-0.5).then_inc(rstd_ready, 1)
                for k in range(KT):
                    act.wait_ge(xn_ready, KT + k + 1)
                    nc.scalar.activation(xhi[:, k], xnb[:, k % 2], ACT.Copy,
                                         scale=par[:, P_FFN + k:P_FFN + k + 1]).then_inc(xhi_ready, 1)
                with act.Fori(0, MF // 2) as j:
                    for b in range(2):
                        act.wait_ge(half_done, half0 + j * 8 + (2 * U_GU + 4 * b + 2))
                        act.wait_ge(acc_free, j * 2 + (N_OUT + b + 1))
                        nc.scalar.activation(halves(sg[:, b]), two_banks(4 * b), ACT.Silu).then_inc(sg_ready, 1)
                        act.wait_ge(acc_free, j * 2 + (2 + N_OUT + b + 1))
                        nc.scalar.activation(hhi[:, bass.ds(j * 2 + b, 1), :].rearrange("p a t -> p (a t)"),
                                             hid[:, b], ACT.Copy).then_inc(hhi_ready, 1)
                act.drain().then_inc(engines_done, 1)
                act.wait_ge(layer_open, l + 1)

        @block.vector
        def _(dve):
            dve.wait_ge(loaded, 48)
            with dve.Fori(0, DEPTH) as l:
                half0 = dve.snap(l * (2 * UNITS) + 4)
                own = [0]

                def chain(ins):
                    own[0] += 1
                    ins.then_inc(dve_step, 1)
                    dve.wait_ge(dve_step, own[0])

                nc.vector.tensor_copy(par[:], par_all[:, bass.ds(l, 1), :].rearrange("p a n -> p (a n)")).then_inc(par_ready, 1)
                nc.vector.tensor_copy(ident16[:], cols(C_ID, BLK, slice(0, BLK))).then_inc(par_ready, 1)
                nc.vector.tensor_copy(causal16[:], cols(C_CAU, BLK, slice(0, BLK))).then_inc(par_ready, 1)
                nc.vector.memset(att[:].rearrange("p a h t -> p (a h t)"), 0.0).then_inc(par_ready, 1)
                dve.wait_ge(par_ready, 4)
                dve.sem_inc(acc_free, 2)

                def wait_done(job):
                    p, n = turn_of(job)
                    dve.wait_ge(job_done[p], n)
                    return 4 + 2 * p, job_taken[p], n

                def prenorm(s, gains, n0):
                    dve.wait_ge(rstd_ready, s + 1)

                    def low(k):
                        dve.wait_ge(xhi_ready, n0 + k + 1)
                        nc.vector.scalar_tensor_tensor(xlo[:, k], xnb[:, k % 2], par[:, gains + k:gains + k + 1],
                                                       xhi[:, k].bitcast(F32), ALU.mult, ALU.subtract).then_inc(x_ready, 1)

                    for k in range(KT):
                        if k >= 2:
                            dve.wait_ge(x_ready, n0 + k - 1)
                        nc.vector.tensor_tensor(xnb[:, k % 2], h[:, k], rnb[:, 0], ALU.mult).then_inc(xn_ready, 1)
                        dve.wait_ge(xn_ready, s * KT + k + 1)
                        if k >= 1:
                            low(k - 1)
                    low(KT - 1)

                def norm(k):
                    n = NORMS[k]
                    dve.wait_ge(rn_ready, n + 1)
                    if k < GV:
                        rows = slice(0, 64) if k == DKIK else slice(0, 128)
                        g = NORMED[k]
                        nc.vector.scalar_tensor_tensor(feat[rows, k], feat[rows, k], par[rows, g:g + 1], rnb[rows, n % 2],
                                                       ALU.mult, ALU.mult).then_inc(normed, 1)
                    else:
                        nc.vector.scalar_tensor_tensor(feat[:, k], feat[:, k], par[:, P_GO:P_GO + 1], rnb[:, n % 2],
                                                       ALU.mult, ALU.mult).then_inc(normed, 1)
                    dve.wait_ge(normed, n + 1)

                def rope(k):
                    b0, taken, n = wait_done(("rope", k))
                    chain(nc.vector.tensor_tensor(xnb[:, 0], feat[:, k], cols(C_COS, N), ALU.mult))
                    nc.vector.tensor_tensor(halves(xnb[:, 1]), two_banks(b0), halves(cols(C_SIN, N)), ALU.mult).then_inc(taken, 1)
                    dve.wait_ge(taken, n)
                    if k == DKIK:
                        chain(nc.vector.tensor_tensor(kk[0:64, 0], xnb[0:64, 0], xnb[0:64, 1], ALU.add))
                        nc.vector.tensor_tensor(kk[64:128, 1], xnb[64:128, 0], xnb[64:128, 1], ALU.add).then_inc(roped, 1)
                    else:
                        nc.vector.tensor_tensor(feat[:, k], xnb[:, 0], xnb[:, 1], ALU.add).then_inc(roped, 1)
                    dve.wait_ge(roped, ROPES[k] + 1)

                def gates():
                    e, z = feat[:, GG:GG + 2], feat[:, GG + 2:GG + 4]
                    dve.wait_ge(gate_ln, 1)
                    chain(nc.vector.scalar_tensor_tensor(z, z, 0.0, e, ALU.min, ALU.subtract))
                    for t in range(2):
                        chain(nc.vector.tensor_tensor_scan(feat[:, GG + t], cols(C_RST, N), feat[:, GG + 2 + t], 0.0,
                                                           ALU.mult, ALU.add))
                    b = e.rearrange("p t (c s) -> p t c s", s=BLK)
                    mid, end = b[:, :, :, BLK // 2 - 1], b[:, :, :, BLK - 1]
                    chain(nc.vector.tensor_tensor(coef[:, :, 0:NB - 1], end[:, :, 0:NB - 1], mid[:, :, 0:NB - 1], ALU.subtract))
                    nc.vector.tensor_tensor(coef[:, :, 0:NB - 1], coef[:, :, 0:NB - 1], mid[:, :, 1:NB], ALU.add).then_inc(decay_arg, 1)
                    for t in range(2):
                        centre = feat[:, GG + t].rearrange("p (c s) -> p c s", s=BLK)[:, :, BLK // 2 - 1:BLK // 2]
                        ins = nc.vector.tensor_tensor(feat[:, GG + 2 + t].rearrange("p (c s) -> p c s", s=BLK),
                                                      feat[:, GG + t].rearrange("p (c s) -> p c s", s=BLK),
                                                      centre.broadcast_to([128, NB, BLK]), ALU.subtract)
                        if t == 0:
                            chain(ins)
                    ins.then_inc(decay_arg, 1)
                    rows = slice(ROW_FF, ROW_FF + 4)
                    dve.wait_ge(gate_ln, 2)
                    chain(nc.vector.scalar_tensor_tensor(xnb[rows, 1], fox_c[rows], 0.0, xnb[rows, 0], ALU.min, ALU.subtract))
                    nc.vector.tensor_tensor_scan(fox_c[rows], cst[rows, C_COS:C_COS + N], xnb[rows, 1], 0.0,
                                                 ALU.mult, ALU.add).then_inc(fox_ready, 1)
                    dve.wait_ge(fox_ready, 1)

                def decays():
                    dve.wait_ge(decay_exp, 2)
                    dve.wait_ge(feat_ready, 2 * (GK + 1) + 2)
                    nc.vector.scalar_tensor_tensor(feat[:, GQ:GQ + 2], feat[:, GQ:GQ + 2], 0.125, feat[:, GG:GG + 2],
                                                   ALU.mult, ALU.mult).then_inc(decayed, 1)
                    nc.vector.tensor_tensor(feat[:, GK:GK + 2], feat[:, GK:GK + 2], feat[:, GG + 2:GG + 4],
                                            ALU.mult).then_inc(decayed, 1)

                def index(i, hd):
                    n = INDEX[(i, hd)]
                    nk = (i + 1) * BLK
                    p, m = turn_of(("index", i, hd))
                    dve.wait_ge(job_taken[p], m)
                    if n == 0:
                        p, m = turn_of(("turn_tile", SMALL))
                        dve.wait_ge(job_taken[p], m)
                    w = tok_small[:, i, ROW_IW + hd:ROW_IW + hd + 1]
                    if hd == 0:
                        ins = nc.vector.tensor_scalar(score[:, 0:nk], relu[:, n % 2, 0:nk], w, None, ALU.mult)
                    else:
                        ins = nc.vector.scalar_tensor_tensor(score[:, 0:nk], relu[:, n % 2, 0:nk], w, score[:, 0:nk],
                                                             ALU.mult, ALU.add)
                    ins.then_inc(index_used, 1)
                    dve.wait_ge(index_used, n + 1)
                    if hd == 3:
                        chain(nc.vector.tensor_tensor(score[:, block_of(i)], score[:, block_of(i)],
                                                      cols(C_CAU, BLK, slice(0, BLK)), ALU.add))

                def topk(i, r0):
                    nk = (i + 1) * BLK
                    for _ in range(2):
                        chain(nc.vector.max(top8[:], score[:, 0:nk]))
                        chain(nc.vector.match_replace(out=score[:, 0:nk], in_to_replace=top8[:],
                                                      in_values=score[:, 0:nk], imm_value=TAKEN))

                def select(i):
                    nk = (i + 1) * BLK
                    if i >= 3:
                        wait_done(("logits", 0, i - 2, 3))
                    chain(nc.vector.tensor_scalar(selb[:, i % 2, 0:nk], score[:, 0:nk], TAKEN / 2, NEG, ALU.is_gt, ALU.mult))
                    nc.vector.tensor_tensor(selb[:, i % 2, block_of(i)], selb[:, i % 2, block_of(i)], causal16[:],
                                            ALU.add).then_inc(selected, 1)
                    dve.wait_ge(selected, i)

                def logits(g, i, hd):
                    b0, taken, _ = wait_done(("logits", g, i, hd))
                    u = LOGITS[(g, i, hd)]
                    nk = (i + 1) * BLK
                    nc.vector.reduce_max(stat[:, 0, u:u + 1], ps[0:BLK, b0 * 512:b0 * 512 + nk], AX.X).then_inc(max_ready, 1)
                    dve.wait_ge(max_ready, 2 * u + 1)
                    nc.vector.tensor_scalar_mul(stat[:, 1, u:u + 1], stat[:, 0, u:u + 1], -0.125).then_inc(max_ready, 1)

                def heads(g, i):
                    u, grp = LOGITS[(g, i, 3)], GROUPS[(g, i)]
                    p, n = turn_of(("logits", g, i, 3))
                    dve.wait_ge(job_taken[p], n)
                    chain(nc.vector.reciprocal(stat[:, 3, u - 3:u + 1], stat[:, 2, u - 3:u + 1]))
                    dve.wait_ge(values_done, u + 1)
                    nc.vector.tensor_tensor(o_tok[:].rearrange("p (h d) -> p h d", h=4),
                                            ps[0:BLK, 3 * 512:3 * 512 + 256].rearrange("p (h d) -> p h d", h=4),
                                            stat[:, 3, u - 3:u + 1].rearrange("p (h a) -> p h a", a=1)
                                            .broadcast_to([BLK, 4, 64]), ALU.mult).then_inc(heads_ready, 1)

                def mixed(g, i):
                    grp = GROUPS[(g, i)]
                    dve.wait_ge(heads_turned, grp + 1)
                    t = DQ if g == 0 else FQ
                    nc.vector.tensor_copy(feat[:, t:t + 2, block_of(i)],
                                          ps[:, 3 * 512:3 * 512 + 2 * BLK].rearrange("p (t q) -> p t q", t=2)).then_inc(mixed_ready, 1)

                def gla_att(c):
                    b0, taken, _ = wait_done(("gla_att", c))
                    tri = cols(C_TRI, BLK, slice(0, BLK)).bitcast(I32).rearrange("p (a t) -> p a t", a=1).broadcast_to([BLK, 2, BLK])
                    for a in range(2):
                        ins = nc.vector.copy_predicated(att[:, a], tri, bank(b0 + a, 2 * BLK, slice(0, BLK))
                                                        .rearrange("p (h t) -> p h t", h=2))
                    ins.then_inc(taken, 1)

                def gla_kv(c):
                    b0, taken, n = wait_done(("gla_kv", c))
                    for hh in range(2):
                        r = head_rows(hh)
                        kv = ps[r, b0 * 512:(b0 + 1) * 512].rearrange("p (t e) -> p t e", t=2)[:, :, hh * 128:(hh + 1) * 128]
                        if c == 0:
                            ins = nc.vector.tensor_copy(state[r], kv)
                        else:
                            ins = nc.vector.tensor_tensor(state[r], state[r], kv, ALU.add)
                        if hh == 0:
                            chain(ins)
                    ins.then_inc(taken, 1)
                    dve.wait_ge(taken, n)
                    dve.wait_ge(decay_exp, 1)
                    nc.vector.tensor_tensor(state[:], state[:], coef[:, :, c:c + 1].broadcast_to([128, 2, 128]),
                                            ALU.mult).then_inc(state_ready, 1)
                    dve.wait_ge(state_ready, c + 1)

                def gla_mix(hd):
                    dve.wait_ge(silu_exp, hd + 1)
                    e = xnb[:, hd % 2]
                    chain(nc.vector.tensor_scalar_add(e, e, 1.0))
                    chain(nc.vector.reciprocal(e, e))
                    chain(nc.vector.tensor_tensor(e, e, feat[:, GG + hd], ALU.mult))
                    nc.vector.tensor_tensor(feat[:, GG + hd], feat[:, GV + hd], e, ALU.mult).then_inc(gla_mixed, 1)

                prenorm(0, P_ATT, 0)
                do = dict(norm=norm, rope=rope, gates=gates, decays=decays, index=index, topk=topk, select=select,
                          logits=logits, heads=heads, mixed=mixed, gla_att=gla_att, gla_kv=gla_kv, gla_mix=gla_mix)
                for step in STEPS:
                    if step[0] in do:
                        do[step[0]](*step[1:])

                dve.wait_ge(gla_mixed, 4)
                dve.wait_ge(mixed_ready, len(GROUPS))
                for m in range(KT):
                    dve.wait_ge(xhi_ready, KT + m + 1)
                    nc.vector.tensor_tensor(xlo[:, m], mix_tile(m), xhi[:, m].bitcast(F32), ALU.subtract).then_inc(x_ready, 1)

                def add_loop(first_half, halves_each, free0):
                    with dve.Fori(0, KT // 2) as j:
                        for b in range(2):
                            dve.wait_ge(half_done, half0 + j * (2 * halves_each) + (first_half + (b + 1) * halves_each))
                            hm = h[:, bass.ds(j * 2 + b, 1), :].rearrange("p a (c t) -> p (a c) t", c=2)
                            nc.vector.tensor_tensor(hm, two_banks(2 * b), hm, ALU.add).then_inc(acc_free, 1)

                add_loop(2 * U_OUT, 2, 2)
                dve.wait_ge(acc_free, 2 + N_OUT)
                prenorm(1, P_FFN, 2 * KT)
                with dve.Fori(0, MF // 2) as j:
                    for b in range(2):
                        dve.wait_ge(sg_ready, j * 2 + (b + 1))
                        dve.wait_ge(half_done, half0 + j * 8 + (2 * U_GU + 4 * b + 4))
                        nc.vector.tensor_tensor(halves(hid[:, b]), halves(sg[:, b]), two_banks(4 * b + 2),
                                                ALU.mult).then_inc(acc_free, 1)
                        dve.wait_ge(hhi_ready, j * 2 + (b + 1))
                        nc.vector.tensor_tensor(hlo[:, bass.ds(j * 2 + b, 1), :].rearrange("p a t -> p (a t)"), hid[:, b],
                                                hhi[:, bass.ds(j * 2 + b, 1), :].rearrange("p a t -> p (a t)").bitcast(F32),
                                                ALU.subtract).then_inc(hid_ready, 1)
                add_loop(2 * U_DN, 6, 2 + N_OUT + MF)
                dve.drain().then_inc(engines_done, 1)
                dve.wait_ge(engines_done, 3)
                dve.sem_clear(layer_sems)
                dve.drain().then_inc(layer_open, 1)


def pack_columns(w):
    k, n = w.shape
    return w.reshape(k // 128, 128, n // 128, 128).transpose(2, 1, 0, 3).reshape(n // 128, 128, k)


def lay_out_weights(w_in, w_out, w_gate_up, w_down):
    edges = np.cumsum([0, 256, 64, 64, 256, 4, 64, 256, 256, 256, 4, 256, 256, 512, 512, 16])
    names = ("dq", "dk", "dv", "iq", "iw", "ik", "fq", "fk", "fv", "ff", "gq", "gk", "gv", "gg", "lr")
    at = {n: slice(edges[i], edges[i + 1]) for i, n in enumerate(names)}
    out = np.zeros((DEPTH, UNITS, 128, D), w_in.dtype)
    for l in range(DEPTH):
        small = np.zeros((D, 128), w_in.dtype)
        for name, row in (("dv", ROW_DV), ("lr", ROW_LR), ("ff", ROW_FF), ("iw", ROW_IW)):
            part = w_in[l][:, at[name]]
            small[:, row:row + part.shape[1]] = part
        parts = [w_in[l][:, at[n]] for n in ("dq", "dk", "ik", "iq")] + [small]
        parts += [w_in[l][:, at[n]] for n in ("fq", "fk", "fv", "gq", "gk", "gv", "gg")]
        out[l, :N_PROJ] = pack_columns(np.concatenate(parts, axis=1))
        out[l, U_OUT:U_GU] = pack_columns(w_out[l])
        out[l, U_GU:U_DN:2] = pack_columns(w_gate_up[l][:, :FF])
        out[l, U_GU + 1:U_DN:2] = pack_columns(w_gate_up[l][:, FF:])
        down = pack_columns(w_down[l])
        for s, kts in enumerate(DN_PARTS):
            a = sum(DN_PARTS[:s]) * 128
            out[l, U_DN + s::3, :, :kts * 128] = down[:, :, a:a + kts * 128]
    return out


def lay_out_params(attn_norm, ffn_norm, dsa_q_norm, dsa_k_norm, fox_q_norm, fox_k_norm, fox_f_bias, gla_gate_w2,
                   gla_gate_b, gla_out_norm):
    p = np.zeros((DEPTH, 128, N_PAR), attn_norm.dtype)
    for l in range(DEPTH):
        p[l, :, P_ATT:P_ATT + KT] = attn_norm[l].reshape(KT, 128).T
        p[l, :, P_FFN:P_FFN + KT] = ffn_norm[l].reshape(KT, 128).T
        for c, g in ((P_DQ, dsa_q_norm), (P_DK, dsa_k_norm), (P_FQ, fox_q_norm), (P_FK, fox_k_norm)):
            p[l, :, c] = np.tile(g[l], 2)
        p[l, :, P_GO] = gla_out_norm[l]
        p[l, :, P_GB:P_GB + 2] = gla_gate_b[l].reshape(2, 128).T
        p[l, ROW_FF:ROW_FF + 4, P_FB] = fox_f_bias[l]
        p[l, ROW_LR:ROW_LR + RANK, P_W2:] = gla_gate_w2[l]
    return p


def shape_constants():
    c = np.zeros((128, N_CST), np.float32)
    c[:, C_ID:C_ID + 128] = np.eye(128)
    c[:, C_ONE:C_ONE + 128] = 1
    c[:64, C_BLK:C_BLK + 64] = 1
    c[64:, C_BLK + 64:C_BLK + 128] = 1
    half = 8
    inv = np.power(np.float32(500000.0), -np.arange(half, dtype=np.float32) * np.float32(2.0) / np.float32(16))
    ang = np.arange(N, dtype=np.float32)[None, :] * inv.astype(np.float32)[:, None]
    c[:, C_COS:C_COS + N] = 1
    for base in (0, 64):
        for j in range(half):
            lo, hi = base + j, base + half + j
            c[hi, C_ROT + lo] = -1
            c[lo, C_ROT + hi] = 1
            for r in (lo, hi):
                c[r, C_COS:C_COS + N] = np.cos(ang[j])
                c[r, C_SIN:C_SIN + N] = np.sin(ang[j])
    c[:, C_RST:C_RST + N] = np.arange(N) % BLK != 0
    q = np.arange(BLK)
    c[:BLK, C_CAU:C_CAU + BLK] = np.where(q[None, :] > q[:, None], NEG, 0)
    c[:BLK, C_TRI:C_TRI + BLK] = q[None, :] >= q[:, None]
    for hd in range(4):
        c[ROW_FF + hd, C_SEL + hd * BLK:C_SEL + (hd + 1) * BLK] = -8
    c[:, C_EPS] = EPS
    return c


def kernel(x, meta_tokens, attn_norm, w_in, dsa_q_norm, dsa_k_norm, fox_q_norm, fox_k_norm, fox_f_bias, gla_gate_w2,
           gla_gate_b, gla_out_norm, w_out, ffn_norm, w_gate_up, w_down):
    import concourse.bacc as bacc
    from concourse.bass_utils import run_bass_kernel_spmd

    a = np.asarray
    arrays = {
        "hT": np.ascontiguousarray(np.concatenate([a(meta_tokens), a(x)[0]], axis=0).T),
        "weights": lay_out_weights(a(w_in), a(w_out), a(w_gate_up), a(w_down)),
        "params": lay_out_params(a(attn_norm), a(ffn_norm), a(dsa_q_norm), a(dsa_k_norm), a(fox_q_norm), a(fox_k_norm),
                                 a(fox_f_bias), a(gla_gate_w2), a(gla_gate_b), a(gla_out_norm)),
        "consts": shape_constants(),
    }
    nc = bacc.Bacc("TRN2", target_bir_lowering=False, num_devices=1)
    args = [nc.dram_tensor(f"in_{n}", v.shape, mybir.dt.from_np(v.dtype), kind="ExternalInput").ap()
            for n, v in arrays.items()]
    out = nc.dram_tensor("out_hT", (D, SEQ), F32, kind="ExternalOutput").ap()
    hybrid_block(nc, *args, out)
    r = run_bass_kernel_spmd(nc, [{f"in_{n}": v for n, v in arrays.items()}], core_ids=[0])
    return np.ascontiguousarray(r.results[0]["out_hT"].T)[None]
```

```python
from contextlib import ExitStack

import numpy as np
import concourse.bass as bass
from concourse import mybir

F32 = mybir.dt.float32
F32R = mybir.dt.float32r
BF16 = mybir.dt.bfloat16
I32 = mybir.dt.int32
ALU = mybir.AluOpType
ACT = mybir.ActivationFunctionType
AX = mybir.AxisListType

DEPTH, D, SEQ, META = 2, 1024, 512, 16
N = META + SEQ
HALF, BLK = N // 2, 88
NB = N // BLK
KT = D // 128
FF = 2816
MF = FF // 128
TOPK = 128
EPS = 1e-6
NEG, TAKEN = -1e30, -3e38
RANK = 16
TAU = 16.0

DQ, DKIK, IQ, SMALL, FQ, FK, FV, GQ, GK, GV, GG = 0, 2, 3, 5, 6, 8, 10, 12, 14, 16, 20
N_PROJ, N_OUT, N_GU, N_DN = 24, KT, 2 * MF, 3 * KT
UNITS = N_PROJ + N_OUT + N_GU + N_DN
U_OUT, U_GU, U_DN = N_PROJ, N_PROJ + N_OUT, N_PROJ + N_OUT + N_GU
DN_PARTS = (8, 8, 6)
ROW_DV, ROW_LR, ROW_FF, ROW_IW = 0, 64, 96, 100

P_ATT, P_FFN, P_DQ, P_DK, P_FQ, P_FK, P_GO, P_GB, P_FB, P_W2 = 0, 8, 16, 17, 18, 19, 20, 21, 23, 24
N_PAR = P_W2 + 256
C_ID, C_ONE, C_BLK, C_ROT, C_COS, C_SIN = 0, 128, 256, 384, 512, 512 + N
C_RST = C_SIN + N
C_CAU = C_RST + N
C_TRI = C_CAU + BLK
C_SEL = C_TRI + BLK
C_EPS = C_SEL + 4 * BLK
N_CST = C_EPS + 1

TOPK_ROUNDS = 1
CHOOSE_TOTAL = (NB - 1) * (4 + TOPK // 8 // TOPK_ROUNDS + 1)
ATTEND_PER_HALF = 5
ATTEND_ORDER = [(0, 0), (0, 1), (1, 5), (1, 4), (0, 2), (1, 3), (0, 3), (1, 2), (0, 4), (1, 1), (0, 5), (1, 0)]
RING = 4
PLACES = (IQ, IQ + 1, SMALL, FV, GV, GV + 1, GV + 2, GV + 3, DQ, DQ + 1, FQ, FQ + 1, GG, GG + 1, GG + 2, GG + 3,
          DKIK, FK, FK + 1, FV + 1, GQ, GQ + 1, GK, GK + 1)


NORMED = {0: P_DQ, 1: P_DQ, 2: P_DK, 6: P_FQ, 7: P_FQ, 8: P_FK, 9: P_FK}
ROPED = (0, 1, 2, 3, 4)


def attention_steps(groups):
    heads = [(g, i, h) for g, i in groups for h in range(4)]
    steps = []
    for n in range(len(heads) + 5):
        if n < len(heads):
            steps.append(("logits", *heads[n]))
        if 0 <= n - 2 < len(heads):
            steps.append(("turn", *heads[n - 2]))
        if n >= 4 and (n - 4) % 4 == 3 and n - 4 < len(heads):
            steps += [("back", *heads[n - 4][:2]), ("mixed", *heads[n - 4][:2])]
        if 0 <= n - 3 < len(heads):
            steps.append(("values", *heads[n - 3]))
            if heads[n - 3][2] == 3:
                steps += [("scale", *heads[n - 3][:2])]
    return steps


def plan():
    steps = []
    for k in range(6):
        steps += [("proj", k, 0)] + ([("prenorm", 0)] if k == 0 else []) + [("proj", k, 1)]
        if k in (0, 1, 2):
            steps += [("square", k)]
        if k in (1, 2, 3):
            steps += [("norm", k - 1)]
        if k >= 3:
            steps += [("rope", (2, 0, 1)[k - 3])] + ([("copies",)] if k == 3 else [])
    steps += [("rope", 3), ("rope", 4), ("turn_tile", SMALL), ("gate", 0), ("gate", 1), ("gates",)]

    choose = []
    for i in range(1, NB):
        choose += [("index", i, h) for h in range(4)]
        choose += [("topk", i, r) for r in range(0, TOPK // 8, TOPK_ROUNDS)] + [("select", i)]
    attend = attention_steps(ATTEND_ORDER)

    after = {k: [] for k in range(6, N_PROJ)}
    for k in (6, 7, 8, 9):
        after[k] += [("square", k)]
        after[k + 1] += [("norm", k)]
    after[11] += [("turn_tile", FV)]
    after[12] += [("turn_tile", FV + 1)]
    after[15] += [("decays",)]
    after[16] += [("turn_k", 0), ("turn_k", 1)]
    for k in range(GV, GV + 4):
        after[k + 1] += [("turn_tile", k)]
    for h in range(3):
        after[GG + h + 1] += [("silu", h)]
    for c in range(3):
        after[GG + 1 + c] += [("gla_att", c), ("gla_out", c), ("gla_kv", c)]

    def may_start(step):
        if step[0] != "logits":
            return True
        g, i = step[1:3]
        return ("turn_tile", FV + 1) in steps if g else (i == 0 or ("select", i) in steps)

    halves = 2 * (N_PROJ - 6)
    n = 0
    for k in range(6, N_PROJ):
        for hf in range(2):
            steps.append(("proj", k, hf))
            if hf == 1:
                steps += after[k]
            n += 1
            while choose and len(choose) > CHOOSE_TOTAL * (1 - n / halves):
                steps.append(choose.pop(0))
            for _ in range(ATTEND_PER_HALF):
                if attend and may_start(attend[0]):
                    steps.append(attend.pop(0))
    tail = [("silu", 3)]
    for c in range(3, NB):
        tail += [("gla_att", c), ("gla_out", c)] + ([("gla_kv", c)] if c < NB - 1 else [])
    for h in range(4):
        tail += [("square", GV + h), ("norm", GV + h), ("gla_mix", h)]
    while tail or attend:
        for q, count in ((attend, 3), (tail, 1)):
            for _ in range(count):
                if q:
                    steps.append(q.pop(0))
    return steps


STEPS = plan()
AUX_KINDS = ("prenorm", "norm", "rope", "turn_tile", "gate", "index", "logits", "turn", "turn_k", "gla_att", "gla_out",
             "gla_kv", "back")
WIDE_KINDS = ("prenorm", "norm", "rope", "turn_tile", "gate", "turn_k", "gla_att", "gla_out")


def ring_places():
    places, last, begun, at = {}, {}, [0] * RING, 0
    for job in [s for s in STEPS if s[0] in AUX_KINDS] + [("prenorm", 1)]:
        width = 2 if job[0] in WIDE_KINDS or (job[0] in ("index", "logits", "turn") and N > 512 and
                                              (job[1] if job[0] == "index" else job[2]) == NB - 1) else 1
        if at + width > RING:
            at = 0
        banks = range(at, at + width)
        before = {}
        for b in banks:
            if b in last:
                first, n = last[b]
                before[first] = max(n, before.get(first, 0))
        begun[at] += 1
        for b in banks:
            last[b] = (at, begun[at])
        places[job] = (at, begun[at], sorted(before.items()))
        at = (at + width) % RING
    return places, begun


AUX, AUX_BEGUN = ring_places()
SQUARES = {s[1]: n for n, s in enumerate([s for s in STEPS if s[0] == "square"])}
LOGITS = {s[1:]: n for n, s in enumerate([s for s in STEPS if s[0] == "logits"])}
GROUPS = {s[1:]: n for n, s in enumerate([s for s in STEPS if s[0] == "scale"])}
GROUP_ORDER = list(GROUPS)
BACKS = {s[1:]: n for n, s in enumerate([s for s in STEPS if s[0] == "back"])}
ROPES = {s[1]: n for n, s in enumerate([s for s in STEPS if s[0] == "rope"])}
NORMS = {s[1]: n for n, s in enumerate([s for s in STEPS if s[0] == "norm"])}
INDEX = {s[1:]: n for n, s in enumerate([s for s in STEPS if s[0] == "index"])}


def turn_of(job):
    return AUX[job][:2]


def hybrid_block(nc, hT, weights, params, consts, out):
    with ExitStack() as ctx:
        def sb(name, shape, dt=F32, scope=ctx):
            return scope.enter_context(nc.sbuf_tensor(name, shape, dt))

        def sem(name):
            return ctx.enter_context(nc.semaphore(name))

        h = sb("h", [128, KT, N])
        xhi = sb("xhi", [128, KT, N], F32R)
        xlo = sb("xlo", [128, KT, N], F32R)
        raw = sb("raw", [128, 2, KT, 128])
        whi = sb("whi", [128, 2, KT, 128], F32R)
        wlo = sb("wlo", [128, 2, KT, 128], F32R)
        cst = sb("cst", [128, N_CST])
        par_all = sb("par_all", [128, DEPTH, N_PAR])
        par = sb("par", [128, N_PAR])
        sqb = sb("sqb", [128, 2, N])
        rnb = sb("rnb", [128, 2, N])
        rstd = sb("rstd", [128, N])
        xnb = sb("xnb", [128, 2, N])
        with ExitStack() as mixers:
            def mb(name, shape, dt=F32):
                return sb(name, shape, dt, mixers)
            with ExitStack() as split_output:
                mix_hi = sb("mix_hi", [128, KT, N], F32R, split_output)
                mix_lo = sb("mix_lo", [128, KT, N], F32R, split_output)
            feat = mb("feat", [128, N_PROJ, N])
            kk = mb("kk", [128, 2, N])
            tok_small = mb("tok_small", [BLK, NB, 128])
            v_fox = mb("v_fox", [BLK, NB, 256])
            v_gla = mb("v_gla", [BLK, NB, 512])
            k_gla = mb("k_gla", [BLK, NB, 256])
            relu = mb("relu", [BLK, 2, N])
            score = mb("score", [BLK, N])
            top8 = mb("top8", [BLK, 8])
            selb = mb("selb", [BLK, 2, N], BF16)
            ident16 = mb("ident16", [BLK, BLK], BF16)
            causal16 = mb("causal16", [BLK, BLK], BF16)
            probs = mb("probs", [BLK, 3, N])
            probs_t = mb("probs_t", [BLK, 2, NB, BLK])
            stat = mb("stat", [BLK, 4, 48])
            o_tok = mb("o_tok", [BLK, 256])
            c16 = mb("c16", [128, N], BF16)
            sel16 = mb("sel16", [128, 4 * BLK], BF16)
            att = mb("att", [BLK, 2, 2, BLK])
            state = mb("state", [128, 2, 128])
            coef = mb("coef", [128, 2, NB])
        with ExitStack() as ffn:
            hhi = sb("hhi", [128, MF, N], F32R, ffn)
            hlo = sb("hlo", [128, MF, N], F32R, ffn)
            sg = sb("sg", [128, 2, N], F32, ffn)
            hid = sb("hid", [128, 2, N], F32, ffn)
        ps = ctx.enter_context(nc.psum_tensor("ps", [128, 8 * 512], F32))

        loaded = sem("loaded")
        h_loaded = [sem(f"h_loaded{k}") for k in range(KT)]
        sq_first = sem("sq_first")
        raw_loaded = [sem("raw_loaded0"), sem("raw_loaded1")]
        hi_done = sem("hi_done")
        split_done = sem("split_done")
        half_done = sem("half_done")
        layer_open = sem("layer_open")
        h_done = sem("h_done")
        stored = sem("stored")
        par_ready = sem("par_ready")
        engines_done = sem("engines_done")
        sq_ready = sem("sq_ready")
        summed = sem("summed")
        rstd_ready = sem("rstd_ready")
        xhi_ready = sem("xhi_ready")
        x_ready = sem("x_ready")
        feat_ready = sem("feat_ready")
        job_done = [sem(f"job_done{b}") for b in range(RING)]
        job_taken = [sem(f"job_taken{b}") for b in range(RING)]
        normed = sem("normed")
        roped = sem("roped")
        copied = sem("copied")
        gate_step = sem("gate_step")
        gate_ln = sem("gate_ln")
        decay_arg = sem("decay_arg")
        decay_exp = sem("decay_exp")
        decayed = sem("decayed")
        fox_ready = sem("fox_ready")
        fox_part = sem("fox_part")
        c16_ready = sem("c16_ready")
        index_used = sem("index_used")
        selected = sem("selected")
        max_ready = sem("max_ready")
        values_done = sem("values_done")
        heads_ready = sem("heads_ready")
        mixed_hi = sem("mixed_hi")
        state_ready = sem("state_ready")
        sigmoid_ready = sem("sigmoid_ready")
        silu_done = sem("silu_done")
        gla_mixed = sem("gla_mixed")
        gla_hi = sem("gla_hi")
        gla_split = sem("gla_split")
        rn_ready = sem("rn_ready")
        acc_free = sem("acc_free")
        gate_scaled = sem("gate_scaled")
        sg_ready = sem("sg_ready")
        hidden = sem("hidden")
        hhi_ready = sem("hhi_ready")
        hid_ready = sem("hid_ready")
        act_step = sem("act_step")
        dve_step = sem("dve_step")
        layer_sems = range(par_ready.num, dve_step.num + 1)

        def cols(base, n, rows=slice(0, 128)):
            return cst[rows, base:base + n]

        def bank(b, n, rows=slice(0, 128)):
            return ps[rows, b * 512:b * 512 + n]

        def two_banks(b):
            return ps[:, b * 512:(b + 2) * 512].rearrange("p (a c) -> p a c", a=2)[:, :, 0:HALF]

        def halves(ap):
            return ap.rearrange("p (a c) -> p a c", a=2)

        def group_waits():
            last = {}
            for s in BACKS:
                p, n = turn_of(("back",) + s)
                last[p] = max(n, last.get(p, 0))
            return [(job_taken[p], n) for p, n in last.items()]

        def block_of(i):
            return slice(i * BLK, (i + 1) * BLK)

        def head_rows(hd):
            return slice(64 * (hd % 2), 64 * (hd % 2) + 64)

        def place(k):
            return PLACES.index(k)

        def pair(k):
            return slice(place(k), place(k) + 2)

        fox_rows = slice(ROW_FF, ROW_FF + 4)

        def part16():
            return xnb[fox_rows, 0].bitcast(BF16)[:, 0:N]

        def fox_gate():
            return feat[fox_rows, place(SMALL)]

        block = ctx.enter_context(nc.Block())

        @block.sync
        def _(sp):
            with sp.Fori(0, DEPTH) as l:
                with sp.Fori(0, UNITS // 2) as j:
                    for b in range(2):
                        sp.wait_ge(split_done, l * UNITS + j * 2 + (b + 1))
                        sp.dma_start(raw[:, b].rearrange("p k n -> p (k n)"),
                                     weights[l, j * 2 + b]).then_inc(raw_loaded[b], 16)
            for k in range(KT):
                sp.wait_ge(h_done, KT * DEPTH + k + 1)
                sp.dma_start(out[k * 128:(k + 1) * 128, :], h[:, k, META:N]).then_inc(stored, 16)
            sp.wait_ge(stored, 16 * KT)

        @block.gpsimd
        def _(pool):
            pool.sem_inc(split_done, 2)
            with pool.Fori(0, DEPTH) as l:
                with pool.Fori(0, UNITS // 2) as j:
                    for b in range(2):
                        pool.wait_ge(hi_done, l * UNITS + j * 2 + (b + 1))
                        nc.gpsimd.tensor_tensor(wlo[:, b], raw[:, b], whi[:, b].bitcast(F32),
                                                ALU.subtract).then_inc(split_done, 1)

        @block.tensor
        def _(pe):
            pe.sem_inc(half_done, 4)
            pe.wait_ge(loaded, 32)
            with pe.Fori(0, DEPTH) as l:
                unit0 = pe.snap(l * UNITS + 2)
                ident, ones = cols(C_ID, 128), cols(C_ONE, 128)
                pe.wait_ge(par_ready, 6)

                def job_begin(job):
                    p, _, before = AUX[job]
                    for q, n in before:
                        pe.wait_ge(job_taken[q], n)
                    return 4 + p, job_done[p]

                def wait_taken(job):
                    p, n = turn_of(job)
                    pe.wait_ge(job_taken[p], n)

                def unit_half(b, bank_no, hf, x, order=range(KT), first=True, last=True, waits={}):
                    for n, k in enumerate(order):
                        for w in waits.get(k, ()):
                            pe.wait_ge(*w)
                        hi, lo = (a[:, hf * HALF:(hf + 1) * HALF] for a in x(k))
                        for t, (w, a) in enumerate(((whi, hi), (whi, lo), (wlo, hi))):
                            ins = nc.tensor.matmul(bank(bank_no, HALF), w[:, b, k % KT], a,
                                                   start=(first and n == 0 and t == 0),
                                                   stop=(last and n == len(order) - 1 and t == 2))
                    ins.then_inc(half_done, 1)

                def x_tiles(k):
                    return xhi[:, k], xlo[:, k]

                def mix_tiles(k):
                    return mix_hi[:, k], mix_lo[:, k]

                def prenorm(s):
                    b0, done = job_begin(("prenorm", s))
                    if s == 0:
                        pe.wait_ge(h_done, l * KT + KT)
                    else:
                        pe.wait_ge(summed, KT)
                    for hf in range(2):
                        ins = nc.tensor.matmul(bank(b0 + hf, HALF), ones, rstd[:, hf * HALF:(hf + 1) * HALF],
                                               start=True, stop=True)
                    ins.then_inc(done, 1)

                def proj(k, hf):
                    q = 2 * k + hf
                    if hf == 0:
                        pe.wait_ge(split_done, unit0 + (k + 1))
                    if q >= 3:
                        pe.wait_ge(feat_ready, q - 2)
                    unit_half(k % 2, q % 3, hf, x_tiles,
                              waits={n: [(x_ready, n + 1)] for n in range(KT)} if q == 0 else {})

                def norm(k):
                    b0, done = job_begin(("norm", k))
                    pe.wait_ge(sq_ready, SQUARES[k] + 1)
                    lhs = cols(C_BLK, 128) if k < GV else ones
                    for hf in range(2):
                        ins = nc.tensor.matmul(bank(b0 + hf, HALF), lhs,
                                               sqb[:, SQUARES[k] % 2, hf * HALF:(hf + 1) * HALF], start=True, stop=True)
                    ins.then_inc(done, 1)

                def rope(k):
                    b0, done = job_begin(("rope", k))
                    if k in NORMS:
                        pe.wait_ge(normed, NORMS[k] + 1)
                    pe.wait_ge(feat_ready, 2 * k + 2)
                    for hf in range(2):
                        ins = nc.tensor.matmul(bank(b0 + hf, HALF), cols(C_ROT, 128),
                                               feat[:, place(k), hf * HALF:(hf + 1) * HALF], start=True, stop=True)
                    ins.then_inc(done, 1)

                def turn_tile(k):
                    b0, done = job_begin(("turn_tile", k))
                    pe.wait_ge(feat_ready, 2 * k + 2)
                    turn_blocks(feat[:, place(k), :], b0, done)

                def turn_k(t):
                    b0, done = job_begin(("turn_k", t))
                    pe.wait_ge(decayed, 2)
                    turn_blocks(feat[:, place(GK + t), :], b0, done)

                def turn_blocks(src, b0, done):
                    for i in range(NB):
                        col = (b0 + i // 3) * 512 + (i % 3) * 128
                        ins = nc.tensor.transpose(ps[0:BLK, col:col + 128], src[:, block_of(i)], ident)
                    ins.then_inc(done, 1)

                def gate(t):
                    b0, done = job_begin(("gate", t))
                    pe.wait_ge(feat_ready, 2 * SMALL + 2)
                    rows = slice(ROW_LR, ROW_LR + RANK)
                    for hf in range(2):
                        ins = nc.tensor.matmul(bank(b0 + hf, HALF), par[rows, P_W2 + t * 128:P_W2 + (t + 1) * 128],
                                               feat[rows, place(SMALL), hf * HALF:(hf + 1) * HALF], start=True, stop=True)
                    ins.then_inc(done, 1)

                def pieces(n):
                    return [(0, min(n, 512))] + ([(512, n)] if n > 512 else [])

                def index(i, hd):
                    b0, done = job_begin(("index", i, hd))
                    if (i, hd) == (1, 0):
                        pe.wait_ge(roped, len(ROPES))
                        pe.wait_ge(copied, 2)
                    r = head_rows(hd)
                    for a, z in pieces((i + 1) * BLK):
                        ins = nc.tensor.matmul(ps[0:BLK, b0 * 512 + a:b0 * 512 + z], feat[r, place(IQ + hd // 2), block_of(i)],
                                               kk[r, 1, a:z], start=True, stop=True)
                    ins.then_inc(done, 1)

                def logits(g, i, hd):
                    b0, done = job_begin(("logits", g, i, hd))
                    r = head_rows(hd)
                    n = (i + 1) * BLK
                    if g == 0:
                        q, key = feat[r, place(DQ + hd // 2), block_of(i)], kk[r, 0, :]
                        if hd == 0:
                            pe.wait_ge(roped, len(ROPES))
                            pe.wait_ge(copied, 2)
                            if i:
                                pe.wait_ge(selected, i)
                    else:
                        q, key = feat[r, place(FQ + hd // 2), block_of(i)], feat[r, place(FK + hd // 2), :]
                        if hd == 0:
                            pe.wait_ge(normed, NORMS[FK + 1] + 1)
                            pe.wait_ge(c16_ready, 3)
                    for a, z in pieces(n):
                        o = ps[0:BLK, b0 * 512 + a:b0 * 512 + z]
                        last = z == n and g == 0 and i > 0
                        ins = nc.tensor.matmul(o, q, key[:, a:z], start=True, stop=False)
                        if g == 1:
                            ins = nc.tensor.matmul(o, sel16[:, hd * BLK:(hd + 1) * BLK], c16[:, a:z],
                                                   start=False, stop=(z <= i * BLK))
                        if g == 0 and i > 0:
                            ins = nc.tensor.matmul(o, ident16[:], selb[:, i % 2, a:z], start=False, stop=True)
                        else:
                            lo = max(a, i * BLK)
                            if z > lo:
                                ins = nc.tensor.matmul(ps[0:BLK, b0 * 512 + lo:b0 * 512 + z], ident16[:],
                                                       causal16[:, lo - i * BLK:z - i * BLK], start=False, stop=True)
                    ins.then_inc(done, 1)

                def turn(g, i, hd):
                    b0, done = job_begin(("turn", g, i, hd))
                    wait_taken(("logits", g, i, hd))
                    u = LOGITS[(g, i, hd)]
                    for j in range(i + 1):
                        col = b0 * 512 + (j * BLK if i < NB - 1 else (j // 3) * 512 + (j % 3) * BLK)
                        ins = nc.tensor.transpose(ps[0:BLK, col:col + BLK], probs[:, u % 3, block_of(j)],
                                                  cols(C_ID, BLK, slice(0, BLK)))
                    ins.then_inc(done, 1)

                def values(g, i, hd):
                    wait_taken(("turn", g, i, hd))
                    u, grp = LOGITS[(g, i, hd)], GROUPS[(g, i)]
                    if hd == 0:
                        if grp:
                            pe.wait_ge(heads_ready, grp)
                        for t in ((SMALL,) if g == 0 else (FV, FV + 1)):
                            wait_taken(("turn_tile", t))
                    for j in range(i + 1):
                        v = tok_small[:, j, 0:64] if g == 0 else v_fox[:, j, hd * 64:(hd + 1) * 64]
                        ins = nc.tensor.matmul(ps[0:BLK, 3 * 512 + hd * 64:3 * 512 + (hd + 1) * 64],
                                               probs_t[:, u % 2, j, :], v, start=(j == 0), stop=(j == i))
                    ins.then_inc(values_done, 1)

                def back(g, i):
                    b0, done = job_begin(("back", g, i))
                    pe.wait_ge(heads_ready, GROUPS[(g, i)] + 1)
                    for t in range(2):
                        ins = nc.tensor.transpose(ps[:, b0 * 512 + t * BLK:b0 * 512 + (t + 1) * BLK],
                                                  o_tok[:, t * 128:(t + 1) * 128], cols(C_ID, BLK, slice(0, BLK)))
                    ins.then_inc(done, 1)

                def gla_place(b0, hd):
                    col = (b0 + hd % 2) * 512 + (hd // 2) * BLK
                    return ps[:, col:col + BLK]

                def gla_att(c):
                    b0, done = job_begin(("gla_att", c))
                    pe.wait_ge(decayed, 2)
                    for hd in range(4):
                        r = head_rows(hd)
                        ins = nc.tensor.matmul(gla_place(b0, hd)[0:BLK],
                                               feat[r, place(GK + hd // 2), block_of(c)], feat[r, place(GQ + hd // 2), block_of(c)],
                                               start=True, stop=True)
                    ins.then_inc(done, 1)

                def gla_out(c):
                    b0, done = job_begin(("gla_out", c))
                    wait_taken(("gla_att", c))
                    if c == 0:
                        for t in range(4):
                            wait_taken(("turn_tile", GV + t))
                    else:
                        pe.wait_ge(state_ready, c)
                    for hd in range(4):
                        r = head_rows(hd)
                        o = gla_place(b0, hd)
                        if c:
                            nc.tensor.matmul(o, state[r, hd // 2, :], feat[r, place(GQ + hd // 2), block_of(c)],
                                             start=True, stop=False)
                        ins = nc.tensor.matmul(o, v_gla[:, c, hd * 128:(hd + 1) * 128], att[:, hd % 2, hd // 2, :],
                                               start=(c == 0), stop=True)
                    ins.then_inc(done, 1)

                def gla_kv(c):
                    b0, done = job_begin(("gla_kv", c))
                    if c == 0:
                        for t in range(2):
                            wait_taken(("turn_k", t))
                    for t in range(2):
                        ins = nc.tensor.matmul(ps[:, b0 * 512 + t * 256:b0 * 512 + (t + 1) * 256],
                                               k_gla[:, c, t * 128:(t + 1) * 128], v_gla[:, c, t * 256:(t + 1) * 256],
                                               start=True, stop=True)
                    ins.then_inc(done, 1)

                do = dict(prenorm=prenorm, proj=proj, norm=norm, rope=rope, turn_tile=turn_tile, turn_k=turn_k, gate=gate,
                          index=index, logits=logits, turn=turn, values=values, back=back, gla_att=gla_att,
                          gla_out=gla_out, gla_kv=gla_kv)
                for step in STEPS:
                    if step[0] in do:
                        do[step[0]](*step[1:])

                pe.wait_ge(feat_ready, 2 * N_PROJ)
                with pe.Fori(0, N_OUT // 2) as j:
                    for b in range(2):
                        pe.wait_ge(split_done, unit0 + j * 2 + (U_OUT + b + 1))
                        pe.wait_ge(acc_free, j * 2 + (b + 1))
                        for hf in range(2):
                            unit_half(b, 2 * b + hf, hf, mix_tiles, order=(4, 5, 6, 7, 0, 1, 2, 3),
                                      waits={4: [(gla_split, 4)], 0: group_waits()} if hf == 0 else {})

                def gate_up(j, b, begin=False):
                    pe.wait_ge(acc_free, j * 2 + (N_OUT + b + 1))
                    for s in range(2):
                        pe.wait_ge(split_done, unit0 + j * 4 + (U_GU + 2 * b + s + 1))
                        for hf in range(2):
                            unit_half(s, 4 * b + 2 * s + hf, hf, x_tiles,
                                      waits={n: [(x_ready, KT + n + 1)] for n in range(KT)} if begin and s == hf == 0 else {})
                        if begin and s == 0:
                            prenorm(1)

                gate_up(0, 0, begin=True)
                for q in range(RING):
                    pe.wait_ge(job_taken[q], AUX_BEGUN[q])
                gate_up(0, 1)
                with pe.Fori(1, MF // 2) as j:
                    for b in range(2):
                        gate_up(j, b)
                pe.wait_ge(hid_ready, MF)
                pe.wait_ge(acc_free, 2 + N_OUT + MF)
                with pe.Fori(0, KT // 2) as j:
                    for b in range(2):
                        pe.wait_ge(acc_free, j * 2 + (N_OUT + MF + b + 1))
                        for s, kts in enumerate(DN_PARTS):
                            pe.wait_ge(split_done, unit0 + j * 6 + (U_DN + 3 * b + s + 1))
                            k0 = sum(DN_PARTS[:s])
                            for hf in range(2):
                                unit_half((3 * b + s) % 2, 2 * b + hf, hf, lambda k: (hhi[:, k], hlo[:, k]),
                                          order=range(k0, k0 + kts), first=(s == 0), last=(s == 2))
                pe.drain().then_inc(engines_done, 1)
                pe.wait_ge(layer_open, l + 1)

        @block.scalar
        def _(act):
            for k in range(KT):
                act.dma_start(h[:, k], hT[k * 128:(k + 1) * 128, :]).then_inc(h_loaded[k], 16)
            act.dma_start(par_all[:], params.rearrange("l p n -> p l n")).then_inc(loaded, 16)
            act.dma_start(cst[:], consts).then_inc(loaded, 16)
            eps = cols(C_EPS, 1)

            def square_of(k, slot):
                return nc.scalar.activation(sqb[:, slot], h[:, k], ACT.Square)

            for k in range(KT):
                act.wait_ge(h_loaded[k], 16)
                if k >= 2:
                    act.wait_ge(h_done, k - 1)
                square_of(k, k % 2).then_inc(sq_first, 1)
            act.wait_ge(loaded, 32)
            with act.Fori(0, DEPTH) as l:
                nc.scalar.preload_act_table_set("natural_log_exp_and_others")
                half0 = act.snap(l * (2 * UNITS) + 4)
                raw0 = act.snap(l * (8 * UNITS))
                own = [0]

                def round_unit(n, slot):
                    act.wait_ge(half_done, half0 + (n * 2 - 2))
                    act.wait_ge(raw_loaded[slot], raw0 + (n - slot) * 8 + 16)
                    nc.scalar.activation(whi[:, slot], raw[:, slot], ACT.Copy).then_inc(hi_done, 1)

                def chain(ins):
                    own[0] += 1
                    ins.then_inc(act_step, 1)
                    act.wait_ge(act_step, own[0])

                def wait_done(job):
                    p, n = turn_of(job)
                    act.wait_ge(job_done[p], n)
                    return 4 + p, job_taken[p], n

                def rsqrt_mean(job, count, dst):
                    b0, taken, n = wait_done(job)
                    nc.scalar.activation(halves(dst), two_banks(b0), ACT.Ln, bias=eps, scale=1.0 / count).then_inc(taken, 1)
                    act.wait_ge(taken, n)

                def prenorm(s):
                    rsqrt_mean(("prenorm", s), D, rstd[:])
                    nc.scalar.activation(rstd[:], rstd[:], ACT.Exp, scale=-0.5).then_inc(rstd_ready, 1)

                def x_high(k, gains):
                    nc.scalar.activation(xhi[:, k], h[:, k], ACT.Copy,
                                         scale=par[:, gains + k:gains + k + 1]).then_inc(xhi_ready, 1)

                def proj(k, hf):
                    if hf == 1:
                        round_unit(k + 2, k % 2)

                def square(k):
                    n = SQUARES[k]
                    if k < GV:
                        act.wait_ge(feat_ready, 2 * k + 2)
                    else:
                        p, m = turn_of(("gla_out", NB - 1))
                        act.wait_ge(job_taken[p], m)
                    if n >= 2:
                        before = [s for s in STEPS if s[0] == "square"][n - 2][1]
                        wait_done(("norm", before))
                    nc.scalar.activation(sqb[:, n % 2], feat[:, place(k)], ACT.Square).then_inc(sq_ready, 1)

                def norm(k):
                    n = NORMS[k]
                    if n >= 2:
                        act.wait_ge(normed, n - 1)
                    dst = rnb[:, n % 2]
                    rsqrt_mean(("norm", k), 64 if k < GV else 128, dst)
                    nc.scalar.activation(dst, dst, ACT.Exp, scale=-0.5).then_inc(rn_ready, 1)

                def copies():
                    act.wait_ge(roped, ROPES[2] + 1)
                    nc.scalar.activation(kk[64:128, 0], kk[0:64, 0], ACT.Copy).then_inc(copied, 1)
                    nc.scalar.activation(kk[0:64, 1], kk[64:128, 1], ACT.Copy).then_inc(copied, 1)

                def take_blocks(job, dst):
                    b0, taken, _ = wait_done(job)
                    src = ps[0:BLK, b0 * 512:(b0 + 2) * 512].rearrange("p (a c) -> p a c", a=2)[:, :, 0:384]
                    nc.scalar.activation(dst.rearrange("p (a i) c -> p a i c", a=2),
                                         src.rearrange("p a (i c) -> p a i c", i=3), ACT.Copy).then_inc(taken, 1)

                def turn_tile(k):
                    take_blocks(("turn_tile", k),
                                tok_small[:] if k == SMALL else
                                v_fox[:, :, (k - FV) * 128:(k - FV + 1) * 128] if k < GV else
                                v_gla[:, :, (k - GV) * 128:(k - GV + 1) * 128])

                def turn_k(t):
                    take_blocks(("turn_k", t), k_gla[:, :, t * 128:(t + 1) * 128])

                def gate(t):
                    b0, taken, _ = wait_done(("gate", t))
                    nc.scalar.activation(halves(feat[:, place(GG + 2 + t)]), two_banks(b0), ACT.Identity,
                                         bias=par[:, P_GB + t:P_GB + t + 1]).then_inc(taken, 1)

                def gates():
                    for t in range(2):
                        p, n = turn_of(("gate", t))
                        act.wait_ge(job_taken[p], n)
                    e = feat[:, pair(GG)]
                    chain(nc.scalar.activation(e, feat[:, pair(GG + 2)], ACT.Abs))
                    chain(nc.scalar.activation(e, e, ACT.Exp, scale=-1.0))
                    nc.scalar.activation(e, e, ACT.Ln, bias=cols(C_ONE, 1)).then_inc(gate_ln, 1)
                    p, n = turn_of(("turn_tile", SMALL))
                    act.wait_ge(job_done[p], n)
                    chain(nc.scalar.activation(fox_gate(), fox_gate(), ACT.Identity, bias=par[fox_rows, P_FB:P_FB + 1]))
                    act.wait_ge(roped, len(ROPES))
                    f = xnb[fox_rows, 0]
                    chain(nc.scalar.activation(f, fox_gate(), ACT.Abs))
                    chain(nc.scalar.activation(f, f, ACT.Exp, scale=-1.0))
                    nc.scalar.activation(f, f, ACT.Ln, bias=cols(C_ONE, 1, fox_rows)).then_inc(gate_ln, 1)
                    act.wait_ge(decay_arg, 1)
                    nc.scalar.activation(coef[:, :, 0:NB - 1], coef[:, :, 0:NB - 1], ACT.Exp, scale=1.0 / TAU).then_inc(decay_exp, 1)
                    act.wait_ge(decay_arg, 2)
                    d = feat[:, pair(GG + 2)]
                    chain(nc.scalar.activation(e, d, ACT.Exp, scale=1.0 / TAU))
                    nc.scalar.activation(d, d, ACT.Exp, scale=-1.0 / TAU).then_inc(decay_exp, 1)
                    act.wait_ge(fox_part, 1)
                    nc.scalar.activation(c16[64:68], part16(), ACT.Copy).then_inc(c16_ready, 1)
                    act.wait_ge(fox_part, 2)
                    nc.scalar.activation(c16[32:36], fox_gate(), ACT.Copy).then_inc(c16_ready, 1)

                def index(i, hd):
                    b0, taken, _ = wait_done(("index", i, hd))
                    n = INDEX[(i, hd)]
                    if n >= 2:
                        act.wait_ge(index_used, n - 1)
                    nk = (i + 1) * BLK
                    nc.scalar.activation(relu[:, n % 2, 0:nk], ps[0:BLK, b0 * 512:b0 * 512 + nk], ACT.Relu,
                                         scale=1.0 / 16).then_inc(taken, 1)

                def logits(g, i, hd):
                    b0, taken, _ = wait_done(("logits", g, i, hd))
                    u = LOGITS[(g, i, hd)]
                    act.wait_ge(max_ready, 2 * u + 2)
                    if u >= 3:
                        before = [s for s in STEPS if s[0] == "logits"][u - 3][1:]
                        wait_done(("turn",) + before)
                    nk = (i + 1) * BLK
                    nc.scalar.activation(probs[:, u % 3, 0:nk], ps[0:BLK, b0 * 512:b0 * 512 + nk], ACT.Exp,
                                         bias=stat[:, 1, u:u + 1], scale=0.125,
                                         accum_out=stat[:, 2, u:u + 1]).then_inc(taken, 1)

                def turn(g, i, hd):
                    b0, taken, _ = wait_done(("turn", g, i, hd))
                    u = LOGITS[(g, i, hd)]
                    if u >= 2:
                        act.wait_ge(values_done, u - 1)
                    if i < NB - 1:
                        nc.scalar.activation(probs_t[:, u % 2, 0:i + 1], ps[0:BLK, b0 * 512:b0 * 512 + (i + 1) * BLK]
                                             .rearrange("p (j q) -> p j q", q=BLK), ACT.Copy).then_inc(taken, 1)
                    else:
                        nc.scalar.activation(probs_t[:, u % 2].rearrange("p (a j) q -> p a (j q)", a=2),
                                             two_banks(b0)[0:BLK], ACT.Copy).then_inc(taken, 1)

                def gla_out(c):
                    b0, taken, _ = wait_done(("gla_out", c))
                    for a in range(2):
                        ins = nc.scalar.activation(feat[:, place(GV + a):place(GV + a) + 3:2, block_of(c)], bank(b0 + a, 2 * BLK)
                                                   .rearrange("p (h t) -> p h t", h=2), ACT.Copy)
                    ins.then_inc(taken, 1)

                def silu(hd):
                    act.wait_ge(feat_ready, 2 * (GG + hd) + 2)
                    if hd >= 2:
                        act.wait_ge(silu_done, hd - 1)
                    else:
                        act.wait_ge(c16_ready, 3)
                        act.wait_ge(roped, len(ROPES))
                    s = xnb[:, hd % 2]
                    chain(nc.scalar.activation(s, feat[:, place(GG + hd)], ACT.Exp, scale=-1.0))
                    chain(nc.scalar.activation(s, s, ACT.Ln, bias=cols(C_ONE, 1)))
                    nc.scalar.activation(s, s, ACT.Exp, scale=-1.0).then_inc(sigmoid_ready, 1)

                def mixed(g, i):
                    b0, _, _ = wait_done(("back", g, i))
                    if g:
                        act.wait_ge(c16_ready, 3)
                    nc.scalar.activation(mix_hi[:, 2 * g:2 * g + 2, block_of(i)],
                                         bank(b0, 2 * BLK).rearrange("p (t q) -> p t q", t=2), ACT.Copy).then_inc(mixed_hi, 1)

                def gla_mix(hd):
                    act.wait_ge(gla_mixed, hd + 1)
                    nc.scalar.activation(mix_hi[:, 4 + hd], feat[:, place(GG + hd)], ACT.Copy).then_inc(gla_hi, 1)

                round_unit(0, 0)
                round_unit(1, 1)
                act.wait_ge(par_ready, 6)
                for k in range(KT):
                    x_high(k, P_ATT)
                do = dict(prenorm=prenorm, proj=proj, square=square, norm=norm, copies=copies, turn_tile=turn_tile,
                          turn_k=turn_k, gate=gate, gates=gates, index=index, logits=logits, turn=turn, mixed=mixed,
                          gla_out=gla_out, silu=silu, gla_mix=gla_mix)
                for step in STEPS:
                    if step[0] in do:
                        do[step[0]](*step[1:])

                for m in range(KT):
                    round_unit(U_OUT + m + 2, m % 2)
                    act.wait_ge(acc_free, 2 + m + 1)
                    x_high(m, P_FFN)
                    if m >= 2:
                        act.wait_ge(summed, m - 1)
                    else:
                        wait_done(("norm", GV + 3))
                    square_of(m, m % 2).then_inc(sq_ready, 1)
                prenorm(1)
                nc.scalar.preload_act_table_set("silu_and_others")
                with act.Fori(0, MF // 2) as j:
                    for b in range(2):
                        round_unit(j * 4 + (U_GU + 2 * b + 2), 0)
                        act.wait_ge(gate_scaled, j * 2 + (b + 1))
                        nc.scalar.activation(sg[:, b], sg[:, b], ACT.Silu).then_inc(sg_ready, 1)
                        round_unit(j * 4 + (U_GU + 2 * b + 3), 1)
                        act.wait_ge(hidden, j * 2 + (b + 1))
                        nc.scalar.activation(hhi[:, bass.ds(j * 2 + b, 1), :].rearrange("p a t -> p (a t)"),
                                             hid[:, b], ACT.Copy).then_inc(hhi_ready, 1)

                def down_tiles(j, last):
                    for b in range(2):
                        for s in range(3):
                            if not (last and 3 * b + s >= 4):
                                round_unit(j * 6 + (U_DN + 3 * b + s + 2), (3 * b + s) % 2)
                        act.wait_ge(acc_free, j * 2 + (3 + N_OUT + MF + b))
                        act.wait_ge(h_done, l * KT + j * 2 + (KT + b - 1))
                        nc.scalar.activation(sqb[:, b], h[:, bass.ds(j * 2 + b, 1), :].rearrange("p a t -> p (a t)"),
                                             ACT.Square).then_inc(sq_ready, 1)

                with act.Fori(0, KT // 2 - 1) as j:
                    down_tiles(j, False)
                down_tiles(KT // 2 - 1, True)
                act.drain().then_inc(engines_done, 1)
                act.wait_ge(layer_open, l + 1)

        @block.vector
        def _(dve):
            for k in range(KT):
                dve.wait_ge(sq_first, k + 1)
                if k:
                    dve.wait_ge(h_done, k)
                    nc.vector.tensor_tensor(rstd[:], rstd[:], sqb[:, k % 2], ALU.add).then_inc(h_done, 1)
                else:
                    nc.vector.tensor_copy(rstd[:], sqb[:, 0]).then_inc(h_done, 1)
            dve.wait_ge(loaded, 32)
            with dve.Fori(0, DEPTH) as l:
                half0 = dve.snap(l * (2 * UNITS) + 4)
                own = [0]

                def chain(ins):
                    own[0] += 1
                    ins.then_inc(dve_step, 1)
                    dve.wait_ge(dve_step, own[0])

                nc.vector.tensor_copy(par[:], par_all[:, bass.ds(l, 1), :].rearrange("p a n -> p (a n)")).then_inc(par_ready, 1)
                nc.vector.tensor_copy(ident16[:], cols(C_ID, BLK, slice(0, BLK))).then_inc(par_ready, 1)
                nc.vector.tensor_copy(causal16[:], cols(C_CAU, BLK, slice(0, BLK))).then_inc(par_ready, 1)
                nc.vector.memset(att[:].rearrange("p a h t -> p (a h t)"), 0.0).then_inc(par_ready, 1)
                nc.vector.memset(c16[:], 0.0).then_inc(par_ready, 1)
                nc.vector.tensor_copy(sel16[:], cols(C_SEL, 4 * BLK)).then_inc(par_ready, 1)
                dve.wait_ge(par_ready, 6)
                dve.sem_inc(acc_free, 2)

                def wait_done(job):
                    p, n = turn_of(job)
                    dve.wait_ge(job_done[p], n)
                    return 4 + p, job_taken[p], n

                def x_low(k, gains, n):
                    dve.wait_ge(xhi_ready, n + 1)
                    nc.vector.scalar_tensor_tensor(xlo[:, k], h[:, k], par[:, gains + k:gains + k + 1],
                                                   xhi[:, k].bitcast(F32), ALU.mult, ALU.subtract).then_inc(x_ready, 1)

                def proj(k, hf):
                    if (k, hf) == (0, 0):
                        dve.wait_ge(rstd_ready, 1)
                    if k == GG and hf == 0:
                        dve.wait_ge(decayed, 2)
                    dve.wait_ge(half_done, half0 + (2 * k + hf + 1))
                    cut = slice(hf * HALF, (hf + 1) * HALF)
                    nc.vector.tensor_tensor(feat[:, place(k), cut], bank((2 * k + hf) % 3, HALF), rstd[:, cut],
                                            ALU.mult).then_inc(feat_ready, 1)

                def norm(k):
                    n = NORMS[k]
                    dve.wait_ge(rn_ready, n + 1)
                    dve.wait_ge(feat_ready, 2 * k + 2 if k < GV else 2 * N_PROJ)
                    if k < GV:
                        rows = slice(0, 64) if k == DKIK else slice(0, 128)
                        g = NORMED[k]
                        nc.vector.scalar_tensor_tensor(feat[rows, place(k)], feat[rows, place(k)], par[rows, g:g + 1], rnb[rows, n % 2],
                                                       ALU.mult, ALU.mult).then_inc(normed, 1)
                    else:
                        nc.vector.scalar_tensor_tensor(feat[:, place(k)], feat[:, place(k)], par[:, P_GO:P_GO + 1], rnb[:, n % 2],
                                                       ALU.mult, ALU.mult).then_inc(normed, 1)
                    dve.wait_ge(normed, n + 1)

                def rope(k):
                    b0, taken, n = wait_done(("rope", k))
                    dve.wait_ge(feat_ready, 2 * k + 2)
                    chain(nc.vector.tensor_tensor(xnb[:, 0], feat[:, place(k)], cols(C_COS, N), ALU.mult))
                    nc.vector.tensor_tensor(halves(xnb[:, 1]), two_banks(b0), halves(cols(C_SIN, N)), ALU.mult).then_inc(taken, 1)
                    dve.wait_ge(taken, n)
                    if k == DKIK:
                        chain(nc.vector.tensor_tensor(kk[0:64, 0], xnb[0:64, 0], xnb[0:64, 1], ALU.add))
                        nc.vector.tensor_tensor(kk[64:128, 1], xnb[64:128, 0], xnb[64:128, 1], ALU.add).then_inc(roped, 1)
                    else:
                        nc.vector.tensor_tensor(feat[:, place(k)], xnb[:, 0], xnb[:, 1], ALU.add).then_inc(roped, 1)
                    dve.wait_ge(roped, ROPES[k] + 1)

                def gates():
                    e, z = feat[:, pair(GG)], feat[:, pair(GG + 2)]
                    dve.wait_ge(gate_ln, 1)
                    chain(nc.vector.scalar_tensor_tensor(z, z, 0.0, e, ALU.min, ALU.subtract))
                    for t in range(2):
                        chain(nc.vector.tensor_tensor_scan(feat[:, place(GG + t)], cols(C_RST, N), feat[:, place(GG + 2 + t)], 0.0,
                                                           ALU.mult, ALU.add))
                    b = e.rearrange("p t (c s) -> p t c s", s=BLK)
                    mid, end = b[:, :, :, BLK // 2 - 1], b[:, :, :, BLK - 1]
                    chain(nc.vector.tensor_tensor(coef[:, :, 0:NB - 1], end[:, :, 0:NB - 1], mid[:, :, 0:NB - 1], ALU.subtract))
                    nc.vector.tensor_tensor(coef[:, :, 0:NB - 1], coef[:, :, 0:NB - 1], mid[:, :, 1:NB], ALU.add).then_inc(decay_arg, 1)
                    for t in range(2):
                        centre = feat[:, place(GG + t)].rearrange("p (c s) -> p c s", s=BLK)[:, :, BLK // 2 - 1:BLK // 2]
                        ins = nc.vector.tensor_tensor(feat[:, place(GG + 2 + t)].rearrange("p (c s) -> p c s", s=BLK),
                                                      feat[:, place(GG + t)].rearrange("p (c s) -> p c s", s=BLK),
                                                      centre.broadcast_to([128, NB, BLK]), ALU.subtract)
                        if t == 0:
                            chain(ins)
                    ins.then_inc(decay_arg, 1)
                    dve.wait_ge(gate_ln, 2)
                    chain(nc.vector.scalar_tensor_tensor(xnb[fox_rows, 1], fox_gate(), 0.0, xnb[fox_rows, 0], ALU.min,
                                                         ALU.subtract))
                    nc.vector.tensor_tensor_scan(fox_gate(), cst[fox_rows, C_COS:C_COS + N], xnb[fox_rows, 1], 0.0,
                                                 ALU.mult, ALU.add).then_inc(fox_ready, 1)
                    dve.wait_ge(fox_ready, 1)
                    nc.vector.tensor_copy(c16[fox_rows], fox_gate()).then_inc(c16_ready, 1)
                    dve.wait_ge(c16_ready, 1)
                    chain(nc.vector.tensor_tensor(fox_gate(), fox_gate(), c16[fox_rows], ALU.subtract))
                    nc.vector.tensor_copy(part16(), fox_gate()).then_inc(fox_part, 1)
                    dve.wait_ge(fox_part, 1)
                    nc.vector.tensor_tensor(fox_gate(), fox_gate(), part16(), ALU.subtract).then_inc(fox_part, 1)

                def decays():
                    dve.wait_ge(decay_exp, 2)
                    dve.wait_ge(feat_ready, 2 * (GK + 1) + 2)
                    nc.vector.scalar_tensor_tensor(feat[:, pair(GQ)], feat[:, pair(GQ)], 0.125, feat[:, pair(GG)],
                                                   ALU.mult, ALU.mult).then_inc(decayed, 1)
                    nc.vector.tensor_tensor(feat[:, pair(GK)], feat[:, pair(GK)], feat[:, pair(GG + 2)],
                                            ALU.mult).then_inc(decayed, 1)

                def index(i, hd):
                    n = INDEX[(i, hd)]
                    nk = (i + 1) * BLK
                    p, m = turn_of(("index", i, hd))
                    dve.wait_ge(job_taken[p], m)
                    if n == 0:
                        p, m = turn_of(("turn_tile", SMALL))
                        dve.wait_ge(job_taken[p], m)
                    w = tok_small[:, i, ROW_IW + hd:ROW_IW + hd + 1]
                    if hd == 0:
                        ins = nc.vector.tensor_scalar(score[:, 0:nk], relu[:, n % 2, 0:nk], w, None, ALU.mult)
                    else:
                        ins = nc.vector.scalar_tensor_tensor(score[:, 0:nk], relu[:, n % 2, 0:nk], w, score[:, 0:nk],
                                                             ALU.mult, ALU.add)
                    ins.then_inc(index_used, 1)
                    dve.wait_ge(index_used, n + 1)
                    if hd == 3:
                        chain(nc.vector.tensor_tensor(score[:, block_of(i)], score[:, block_of(i)],
                                                      cols(C_CAU, BLK, slice(0, BLK)), ALU.add))

                def topk(i, r0):
                    nk = (i + 1) * BLK
                    for _ in range(TOPK_ROUNDS):
                        chain(nc.vector.max(top8[:], score[:, 0:nk]))
                        chain(nc.vector.match_replace(out=score[:, 0:nk], in_to_replace=top8[:],
                                                      in_values=score[:, 0:nk], imm_value=TAKEN))

                def select(i):
                    nk = (i + 1) * BLK
                    if i >= 3:
                        wait_done(("logits", 0, i - 2, 3))
                    chain(nc.vector.tensor_scalar(selb[:, i % 2, 0:nk], score[:, 0:nk], TAKEN / 2, NEG, ALU.is_gt, ALU.mult))
                    nc.vector.tensor_tensor(selb[:, i % 2, block_of(i)], selb[:, i % 2, block_of(i)], causal16[:],
                                            ALU.add).then_inc(selected, 1)
                    dve.wait_ge(selected, i)

                def logits(g, i, hd):
                    b0, taken, _ = wait_done(("logits", g, i, hd))
                    u = LOGITS[(g, i, hd)]
                    nk = (i + 1) * BLK
                    nc.vector.reduce_max(stat[:, 0, u:u + 1], ps[0:BLK, b0 * 512:b0 * 512 + nk], AX.X).then_inc(max_ready, 1)
                    dve.wait_ge(max_ready, 2 * u + 1)
                    nc.vector.tensor_scalar_mul(stat[:, 1, u:u + 1], stat[:, 0, u:u + 1], -0.125).then_inc(max_ready, 1)

                def scale(g, i):
                    u, grp = LOGITS[(g, i, 3)], GROUPS[(g, i)]
                    p, n = turn_of(("logits", g, i, 3))
                    dve.wait_ge(job_taken[p], n)
                    if grp:
                        wait_done(("back",) + GROUP_ORDER[grp - 1])
                    chain(nc.vector.reciprocal(stat[:, 3, u - 3:u + 1], stat[:, 2, u - 3:u + 1]))
                    dve.wait_ge(values_done, u + 1)
                    nc.vector.tensor_tensor(o_tok[:].rearrange("p (h d) -> p h d", h=4),
                                            ps[0:BLK, 3 * 512:3 * 512 + 256].rearrange("p (h d) -> p h d", h=4),
                                            stat[:, 3, u - 3:u + 1].rearrange("p (h a) -> p h a", a=1)
                                            .broadcast_to([BLK, 4, 64]), ALU.mult).then_inc(heads_ready, 1)

                def mixed(g, i):
                    dve.wait_ge(mixed_hi, BACKS[(g, i)] + 1)
                    b0, taken, _ = wait_done(("back", g, i))
                    tiles = slice(2 * g, 2 * g + 2)
                    nc.vector.tensor_tensor(mix_lo[:, tiles, block_of(i)],
                                            bank(b0, 2 * BLK).rearrange("p (t q) -> p t q", t=2),
                                            mix_hi[:, tiles, block_of(i)].bitcast(F32), ALU.subtract).then_inc(taken, 1)

                def gla_att(c):
                    b0, taken, _ = wait_done(("gla_att", c))
                    tri = cols(C_TRI, BLK, slice(0, BLK)).bitcast(I32).rearrange("p (a t) -> p a t", a=1).broadcast_to([BLK, 2, BLK])
                    for a in range(2):
                        ins = nc.vector.copy_predicated(att[:, a], tri, bank(b0 + a, 2 * BLK, slice(0, BLK))
                                                        .rearrange("p (h t) -> p h t", h=2))
                    ins.then_inc(taken, 1)

                def gla_kv(c):
                    b0, taken, n = wait_done(("gla_kv", c))
                    for hh in range(2):
                        r = head_rows(hh)
                        kv = ps[r, b0 * 512:(b0 + 1) * 512].rearrange("p (t e) -> p t e", t=2)[:, :, hh * 128:(hh + 1) * 128]
                        if c == 0:
                            ins = nc.vector.tensor_copy(state[r], kv)
                        else:
                            ins = nc.vector.tensor_tensor(state[r], state[r], kv, ALU.add)
                        if hh == 0:
                            chain(ins)
                    ins.then_inc(taken, 1)
                    dve.wait_ge(taken, n)
                    dve.wait_ge(decay_exp, 1)
                    nc.vector.tensor_tensor(state[:], state[:], coef[:, :, c:c + 1].broadcast_to([128, 2, 128]),
                                            ALU.mult).then_inc(state_ready, 1)
                    dve.wait_ge(state_ready, c + 1)

                def silu(hd):
                    dve.wait_ge(sigmoid_ready, hd + 1)
                    dve.wait_ge(feat_ready, 2 * (GG + hd) + 2)
                    nc.vector.tensor_tensor(feat[:, place(GG + hd)], feat[:, place(GG + hd)], xnb[:, hd % 2], ALU.mult).then_inc(silu_done, 1)

                def gla_mix(hd):
                    dve.wait_ge(silu_done, 4)
                    nc.vector.tensor_tensor(feat[:, place(GG + hd)], feat[:, place(GV + hd)], feat[:, place(GG + hd)], ALU.mult).then_inc(gla_mixed, 1)
                    dve.wait_ge(gla_mixed, hd + 1)
                    dve.wait_ge(gla_hi, hd + 1)
                    nc.vector.tensor_tensor(mix_lo[:, 4 + hd], feat[:, place(GG + hd)], mix_hi[:, 4 + hd].bitcast(F32),
                                            ALU.subtract).then_inc(gla_split, 1)

                for k in range(KT):
                    x_low(k, P_ATT, k)
                do = dict(proj=proj, norm=norm, rope=rope, gates=gates, decays=decays, index=index, topk=topk,
                          select=select, logits=logits, scale=scale, mixed=mixed, gla_att=gla_att, gla_kv=gla_kv,
                          silu=silu, gla_mix=gla_mix)
                for step in STEPS:
                    if step[0] in do:
                        do[step[0]](*step[1:])

                chain(nc.vector.memset(rstd[:], 0.0))
                for m in range(KT):
                    dve.wait_ge(half_done, half0 + 2 * (U_OUT + m + 1))
                    nc.vector.tensor_tensor(halves(h[:, m]), two_banks(2 * (m % 2)), halves(h[:, m]), ALU.add).then_inc(acc_free, 1)
                    dve.wait_ge(acc_free, 2 + m + 1)
                    x_low(m, P_FFN, KT + m)
                    dve.wait_ge(sq_ready, len(SQUARES) + m + 1)
                    if m:
                        dve.wait_ge(summed, m)
                    nc.vector.tensor_tensor(rstd[:], rstd[:], sqb[:, m % 2], ALU.add).then_inc(summed, 1)
                dve.wait_ge(rstd_ready, 2)
                with dve.Fori(0, MF // 2) as j:
                    for b in range(2):
                        dve.wait_ge(half_done, half0 + j * 8 + (2 * U_GU + 4 * b + 2))
                        nc.vector.tensor_tensor(halves(sg[:, b]), two_banks(4 * b), halves(rstd[:]),
                                                ALU.mult).then_inc(gate_scaled, 1)
                        dve.wait_ge(half_done, half0 + j * 8 + (2 * U_GU + 4 * b + 4))
                        nc.vector.tensor_tensor(halves(hid[:, b]), two_banks(4 * b + 2), halves(rstd[:]),
                                                ALU.mult).then_inc(acc_free, 1)
                        dve.wait_ge(acc_free, j * 2 + (2 + N_OUT + b + 1))
                        dve.wait_ge(sg_ready, j * 2 + (b + 1))
                        nc.vector.tensor_tensor(hid[:, b], hid[:, b], sg[:, b], ALU.mult).then_inc(hidden, 1)
                        dve.wait_ge(hhi_ready, j * 2 + (b + 1))
                        nc.vector.tensor_tensor(hlo[:, bass.ds(j * 2 + b, 1), :].rearrange("p a t -> p (a t)"), hid[:, b],
                                                hhi[:, bass.ds(j * 2 + b, 1), :].rearrange("p a t -> p (a t)").bitcast(F32),
                                                ALU.subtract).then_inc(hid_ready, 1)

                chain(nc.vector.memset(rstd[:], 0.0))
                with dve.Fori(0, KT // 2) as j:
                    for b in range(2):
                        dve.wait_ge(half_done, half0 + j * 12 + (2 * U_DN + (b + 1) * 6))
                        hm = h[:, bass.ds(j * 2 + b, 1), :].rearrange("p a (c t) -> p (a c) t", c=2)
                        nc.vector.tensor_tensor(hm, two_banks(2 * b), hm, ALU.add).then_inc(acc_free, 1)
                        dve.wait_ge(sq_ready, j * 2 + (len(SQUARES) + KT + b + 1))
                        dve.wait_ge(h_done, l * KT + j * 2 + (KT + b))
                        nc.vector.tensor_tensor(rstd[:], rstd[:], sqb[:, b], ALU.add).then_inc(h_done, 1)
                dve.drain().then_inc(engines_done, 1)
                dve.wait_ge(engines_done, 3)
                dve.sem_clear(layer_sems)
                dve.drain().then_inc(layer_open, 1)


def pack_columns(w):
    k, n = w.shape
    return w.reshape(k // 128, 128, n // 128, 128).transpose(2, 1, 0, 3).reshape(n // 128, 128, k)


def lay_out_weights(w_in, w_out, w_gate_up, w_down):
    edges = np.cumsum([0, 256, 64, 64, 256, 4, 64, 256, 256, 256, 4, 256, 256, 512, 512, 16])
    names = ("dq", "dk", "dv", "iq", "iw", "ik", "fq", "fk", "fv", "ff", "gq", "gk", "gv", "gg", "lr")
    at = {n: slice(edges[i], edges[i + 1]) for i, n in enumerate(names)}
    out = np.zeros((DEPTH, UNITS, 128, D), w_in.dtype)
    for l in range(DEPTH):
        small = np.zeros((D, 128), w_in.dtype)
        for name, row in (("dv", ROW_DV), ("lr", ROW_LR), ("ff", ROW_FF), ("iw", ROW_IW)):
            part = w_in[l][:, at[name]]
            small[:, row:row + part.shape[1]] = part
        parts = [w_in[l][:, at[n]] for n in ("dq", "dk", "ik", "iq")] + [small]
        parts += [w_in[l][:, at[n]] for n in ("fq", "fk", "fv", "gq", "gk", "gv", "gg")]
        out[l, :N_PROJ] = pack_columns(np.concatenate(parts, axis=1))
        out[l, U_OUT:U_GU] = pack_columns(w_out[l])
        out[l, U_GU:U_DN:2] = pack_columns(w_gate_up[l][:, :FF])
        out[l, U_GU + 1:U_DN:2] = pack_columns(w_gate_up[l][:, FF:])
        down = pack_columns(w_down[l])
        for s, kts in enumerate(DN_PARTS):
            a = sum(DN_PARTS[:s]) * 128
            out[l, U_DN + s::3, :, :kts * 128] = down[:, :, a:a + kts * 128]
    return out


def lay_out_params(attn_norm, ffn_norm, dsa_q_norm, dsa_k_norm, fox_q_norm, fox_k_norm, fox_f_bias, gla_gate_w2,
                   gla_gate_b, gla_out_norm):
    p = np.zeros((DEPTH, 128, N_PAR), attn_norm.dtype)
    for l in range(DEPTH):
        p[l, :, P_ATT:P_ATT + KT] = attn_norm[l].reshape(KT, 128).T
        p[l, :, P_FFN:P_FFN + KT] = ffn_norm[l].reshape(KT, 128).T
        for c, g in ((P_DQ, dsa_q_norm), (P_DK, dsa_k_norm), (P_FQ, fox_q_norm), (P_FK, fox_k_norm)):
            p[l, :, c] = np.tile(g[l], 2)
        p[l, :, P_GO] = gla_out_norm[l]
        p[l, :, P_GB:P_GB + 2] = gla_gate_b[l].reshape(2, 128).T
        p[l, ROW_FF:ROW_FF + 4, P_FB] = fox_f_bias[l]
        p[l, ROW_LR:ROW_LR + RANK, P_W2:] = gla_gate_w2[l]
    return p


def shape_constants():
    c = np.zeros((128, N_CST), np.float32)
    c[:, C_ID:C_ID + 128] = np.eye(128)
    c[:, C_ONE:C_ONE + 128] = 1
    c[:64, C_BLK:C_BLK + 64] = 1
    c[64:, C_BLK + 64:C_BLK + 128] = 1
    half = 8
    inv = np.power(np.float32(500000.0), -np.arange(half, dtype=np.float32) * np.float32(2.0) / np.float32(16))
    ang = np.arange(N, dtype=np.float32)[None, :] * inv.astype(np.float32)[:, None]
    c[:, C_COS:C_COS + N] = 1
    for base in (0, 64):
        for j in range(half):
            lo, hi = base + j, base + half + j
            c[hi, C_ROT + lo] = -1
            c[lo, C_ROT + hi] = 1
            for r in (lo, hi):
                c[r, C_COS:C_COS + N] = np.cos(ang[j])
                c[r, C_SIN:C_SIN + N] = np.sin(ang[j])
    c[:, C_RST:C_RST + N] = np.arange(N) % BLK != 0
    q = np.arange(BLK)
    c[:BLK, C_CAU:C_CAU + BLK] = np.where(q[None, :] > q[:, None], NEG, 0)
    c[:BLK, C_TRI:C_TRI + BLK] = q[None, :] >= q[:, None]
    for hd in range(4):
        for row in (32, 64, ROW_FF):
            c[row + hd, C_SEL + hd * BLK:C_SEL + (hd + 1) * BLK] = -8
    c[:, C_EPS] = EPS
    return c


def kernel(x, meta_tokens, attn_norm, w_in, dsa_q_norm, dsa_k_norm, fox_q_norm, fox_k_norm, fox_f_bias, gla_gate_w2,
           gla_gate_b, gla_out_norm, w_out, ffn_norm, w_gate_up, w_down):
    import concourse.bacc as bacc
    from concourse.bass_utils import run_bass_kernel_spmd

    a = np.asarray
    arrays = {
        "hT": np.ascontiguousarray(np.concatenate([a(meta_tokens), a(x)[0]], axis=0).T),
        "weights": lay_out_weights(a(w_in), a(w_out), a(w_gate_up), a(w_down)),
        "params": lay_out_params(a(attn_norm), a(ffn_norm), a(dsa_q_norm), a(dsa_k_norm), a(fox_q_norm), a(fox_k_norm),
                                 a(fox_f_bias), a(gla_gate_w2), a(gla_gate_b), a(gla_out_norm)),
        "consts": shape_constants(),
    }
    nc = bacc.Bacc("TRN2", target_bir_lowering=False, num_devices=1)
    args = [nc.dram_tensor(f"in_{n}", v.shape, mybir.dt.from_np(v.dtype), kind="ExternalInput").ap()
            for n, v in arrays.items()]
    out = nc.dram_tensor("out_hT", (D, SEQ), F32, kind="ExternalOutput").ap()
    hybrid_block(nc, *args, out)
    r = run_bass_kernel_spmd(nc, [{f"in_{n}": v for n, v in arrays.items()}], core_ids=[0])
    return np.ascontiguousarray(r.results[0]["out_hT"].T)[None]
```

```python
from contextlib import ExitStack

import numpy as np
import concourse.bass as bass
from concourse import mybir

F32 = mybir.dt.float32
F32R = mybir.dt.float32r
BF16 = mybir.dt.bfloat16
I32 = mybir.dt.int32
ALU = mybir.AluOpType
ACT = mybir.ActivationFunctionType
AX = mybir.AxisListType

DEPTH, D, SEQ, META = 2, 1024, 512, 16
NB = 5
BLK = -(-(META + SEQ) // NB)
N = -(-NB * BLK // 4) * 4
HALF = N // 2
KT = D // 128
FF = 2816
MF = FF // 128
TOPK = 128
EPS = 1e-6
NEG, TAKEN = -1e30, -3e38
RANK = 16
TAU = 16.0

DQ, DKIK, IQ, SMALL, FQ, FK, FV, GQ, GK, GV, GG = 0, 2, 3, 5, 6, 8, 10, 12, 14, 16, 20
N_PROJ, N_OUT, N_GU, N_DN = 24, KT, 2 * MF, 3 * KT
UNITS = N_PROJ + N_OUT + N_GU + N_DN
U_OUT, U_GU, U_DN = N_PROJ, N_PROJ + N_OUT, N_PROJ + N_OUT + N_GU
STREAM = DEPTH * UNITS + 2
DN_PARTS = (8, 8, 6)
ROW_DV, ROW_LR, ROW_FF, ROW_IW = 0, 64, 96, 100

P_ATT, P_FFN, P_DQ, P_DK, P_FQ, P_FK, P_GO, P_GB, P_FB, P_W2 = 0, 8, 16, 17, 18, 19, 20, 21, 23, 24
P_NEXT = P_W2 + 256
N_PAR = P_NEXT + KT
C_ID, C_ONE, C_BLK, C_ROT, C_COS, C_SIN = 0, 128, 256, 384, 512, 512 + N
C_RST = C_SIN + N
C_CAU = C_RST + N
C_TRI = C_CAU + BLK
C_SEL = C_TRI + BLK
C_EPS = C_SEL + 4
N_CST = C_EPS + 1

TOPK_ROUNDS = 1
STATS = 24
RING = 4
PLACES = (IQ, IQ + 1, SMALL, FV, GV, GV + 1, GV + 2, GV + 3, DQ, DQ + 1, FQ, FQ + 1, GG, GG + 1, GG + 2, GG + 3,
          DKIK, FK, FK + 1, FV + 1, GQ, GQ + 1, GK, GK + 1)


NORMED = {0: P_DQ, 1: P_DQ, 2: P_DK, 6: P_FQ, 7: P_FQ, 8: P_FK, 9: P_FK}
ROPED = (0, 1, 2, 3, 4)


ATTEND_ORDER = [(0, 0), (1, 0), (0, 1), (1, 4), (0, 2), (1, 3), (0, 3), (1, 2), (0, 4), (1, 1)]
AUX_KINDS = ("prenorm", "norm", "rope", "turn_tile", "gate", "index", "logits", "turn", "turn_k", "gla_att", "gla_out",
             "gla_kv", "back")
WIDE_KINDS = ("prenorm", "norm", "rope", "turn_tile", "gate", "turn_k", "gla_att", "gla_out")


class Ring:

    def __init__(self):
        self.last, self.begun, self.at = {}, [0] * RING, 0

    def next_place(self, job):
        block = job[1] if job[0] == "index" else job[2] if job[0] in ("logits", "turn") else 0
        width = 2 if job[0] in WIDE_KINDS or (block + 1) * BLK > 512 else 1
        at = self.at if self.at + width <= RING else 0
        before = {}
        for b in range(at, at + width):
            if b in self.last:
                first, n = self.last[b]
                before[first] = max(n, before.get(first, 0))
        return at, width, before

    def take(self, job):
        at, width, before = self.next_place(job)
        self.begun[at] += 1
        for b in range(at, at + width):
            self.last[b] = (at, self.begun[at])
        self.at = (at + width) % RING
        return at, self.begun[at], sorted(before.items())


def stages(step):
    def pe(columns, count=1, passes=4):
        return ("PE", count * (0.03 + passes * columns / 2400))

    def act(columns, count=1):
        return ("ACT", count * (0.12 + columns / 1200))

    def dve(columns, count=1):
        return ("DVE", count * (0.16 + columns / 960))

    kind = step[0]
    keys = (step[{"index": 1, "topk": 1, "select": 1, "logits": 2, "turn": 2, "values": 2}[kind]] + 1) * BLK \
        if kind in ("index", "topk", "select", "logits", "turn", "values") else 0
    return {
        "proj": lambda: [("PE", 2.65), dve(HALF)] + ([act(D)] if step[2] else []),
        "prenorm": lambda: [pe(HALF, 2), act(N, 2)],
        "square": lambda: [act(N)],
        "norm": lambda: [pe(HALF, 2), act(N, 2), dve(N)],
        "rope": lambda: [pe(HALF, 2), dve(N, 3)],
        "copies": lambda: [act(N, 2)],
        "turn_tile": lambda: [pe(128, NB, 1), act(128 * NB)],
        "turn_k": lambda: [pe(128, NB, 1), act(128 * NB)],
        "gate": lambda: [pe(HALF, 2), act(N)],
        "gate_log": lambda: [act(2 * N, 3), dve(2 * N, 3)],
        "gate_exp": lambda: [act(2 * N, 2)],
        "fox_log": lambda: [act(N, 4), dve(N, 5)],
        "fox_parts": lambda: [act(N, 2)],
        "index": lambda: [pe(keys), act(keys), dve(keys)],
        "topk": lambda: [dve(keys, 2 * TOPK_ROUNDS)],
        "select": lambda: [dve(keys)],
        "logits": lambda: [pe(keys, 1, 5.5), dve(keys), act(keys)],
        "turn": lambda: [pe(keys, 1, 2.2), act(keys)],
        "values": lambda: [("PE", 0.14 * keys / BLK)],
        "scale": lambda: [dve(256)],
        "back": lambda: [pe(BLK, 2, 1)],
        "mixed": lambda: [act(2 * BLK), dve(2 * BLK)],
        "decays": lambda: [dve(2 * N, 2)],
        "gla_att": lambda: [pe(BLK, 4), dve(2 * BLK, 2)],
        "gla_kv": lambda: [pe(256, 2), dve(256, 3)],
        "gla_out": lambda: [pe(BLK, 8), act(2 * BLK, 2)],
        "silu": lambda: [act(N, 3), dve(N)],
        "gla_mix": lambda: [dve(N), act(N), dve(N)],
    }[kind]()


def needs(step, heads, normed):
    kind, k = step[0], step[1] if len(step) > 1 else None
    ropes = [("rope", n) for n in ROPED] + [("copies",)]
    if kind == "proj":
        q = 2 * k + step[2]
        return ([("prenorm", 0), ("proj", (q - 3) // 2, (q - 3) % 2)] if q >= 3 else []) + ([("decays",)] if k >= GG else [])
    if kind == "prenorm":
        return [("proj", 0, 0)]
    if kind == "square":
        n = normed.index(k)
        return [("prenorm", 0), ("gla_out", NB - 1) if k >= GV else ("proj", k, 1)] + ([("norm", normed[n - 2])] if n >= 2 else [])
    if kind == "norm":
        return [("square", k)]
    if kind == "rope":
        return [("proj", k, 1)] + ([("norm", k)] if k in NORMED else [])
    if kind == "copies":
        return [("rope", DKIK)]
    if kind == "turn_tile":
        return [("proj", k, 1)]
    if kind == "turn_k":
        return [("decays",)]
    if kind == "gate":
        return [("proj", SMALL, 1)]
    if kind == "gate_log":
        return [("gate", 0), ("gate", 1)]
    if kind == "gate_exp":
        return [("gate_log",)]
    if kind == "fox_log":
        return [("turn_tile", SMALL)] + ropes
    if kind == "fox_parts":
        return [("fox_log",)]
    if kind == "index":
        return [("turn_tile", SMALL)] + ropes + ([("select", k - 2)] if k >= 3 else [])
    if kind == "topk":
        return [("index", k, 3)]
    if kind == "select":
        return [("logits", 0, k - 2, 3)] if k >= 3 else []
    if kind == "decays":
        return [("gate_exp",), ("proj", GK + 1, 1)]
    if kind == "gla_att":
        return [("decays",)] + ([("gla_out", k - 2)] if k >= 2 else [])
    if kind == "gla_kv":
        return [("turn_k", t) for t in range(2)] + [("turn_tile", GV + t) for t in range(4)] + \
            ([("gla_out", k - 1)] if k else [])
    if kind == "gla_out":
        return [("gla_att", k), ("gla_kv", k - 1) if k else ("turn_tile", GV + 3)]
    if kind == "silu":
        return [("proj", GG + k, 1), ("fox_parts",)] + ropes
    if kind == "gla_mix":
        return [("norm", GV + k)] + [("silu", h) for h in range(4)]
    if kind in ("logits", "turn", "values"):
        g, i, h = step[1:]
        n = heads.index((g, i, h))
        if kind == "logits":
            ready = ([("norm", FK + 1), ("fox_parts",)] if g else ropes + ([("select", i)] if i else []))
            return ready + ([("turn", *heads[n - 3])] if n >= 3 else [])
        if kind == "turn":
            return [("logits", g, i, h)] + ([("values", *heads[n - 2])] if n >= 2 else [])
        ready = [("turn_tile", t) for t in ((FV, FV + 1) if g else (SMALL,))]
        return ready + [("turn", g, i, h)] + ([("scale", *heads[n - 1][:2])] if h == 0 and n else [])
    if kind in ("scale", "back", "mixed"):
        n = ATTEND_ORDER.index(step[1:])
        return {"scale": [("values", *step[1:], 3)] + ([("back", *ATTEND_ORDER[n - 1])] if n else []),
                "back": [("scale", *step[1:])], "mixed": [("back", *step[1:]), ("fox_parts",)]}[kind]
    return []


SLACK_US = 1.9
STALL_US = 0.25


def plan():
    normed = [DQ, DQ + 1, DKIK, FQ, FQ + 1, FK, FK + 1] + [GV + h for h in range(4)]
    heads = [(g, i, h) for g, i in ATTEND_ORDER for h in range(4)]
    choose = []
    for i in range(1, NB):
        choose += [("topk", i, r) for r in range(0, TOPK // 8, TOPK_ROUNDS)] + [("select", i)]
    chains = {
        "values": [("values", *h) for h in heads],
        "scale": [("scale", *a) for a in ATTEND_ORDER],
        "back": [("back", *a) for a in ATTEND_ORDER],
        "mixed": [("mixed", *a) for a in ATTEND_ORDER],
        "turn": [("turn", *h) for h in heads],
        "square": [("square", k) for k in normed],
        "norm": [("prenorm", 0)] + [("norm", k) for k in normed],
        "rope": [("rope", k) for k in (DKIK, DQ, DQ + 1, IQ, IQ + 1)],
        "copies": [("copies",)],
        "turn_tile": [("turn_tile", k) for k in (SMALL, FV, FV + 1, GV, GV + 1, GV + 2, GV + 3)],
        "index": [("index", i, h) for i in range(1, NB) for h in range(4)],
        "choose": choose,
        "fox": [("fox_log",), ("fox_parts",)],
        "gate": [("gate", 0), ("gate", 1), ("gate_log",), ("gate_exp",), ("decays",), ("turn_k", 0), ("turn_k", 1)],
        "gla_out": [("gla_out", c) for c in range(NB)],
        "gla_kv": [("gla_kv", c) for c in range(NB - 1)],
        "gla_att": [("gla_att", c) for c in range(NB)],
        "silu": [("silu", h) for h in range(4)],
        "gla_mix": [("gla_mix", h) for h in range(4)],
        "proj": [("proj", k, hf) for k in range(N_PROJ) for hf in range(2)],
        "logits": [("logits", *h) for h in heads],
    }
    steps, end, taken, backs, free, ring = [], {}, {}, {}, {"PE": 0.0, "ACT": 0.0, "DVE": 0.0}, Ring()
    rounded = {0: 0.0, 1: 0.0}

    def begin(step):
        required = needs(step, heads, normed)
        if any(r not in end for r in required):
            return None
        t = max([end[r] + 0.1 for r in required], default=0.0)
        if step[0] in AUX_KINDS:
            before = ring.next_place(step)[2].items()
            if any(b not in taken for b in before):
                return None
            t = max([t] + [taken[b] + 0.1 for b in before])
        if step[0] == "proj":
            t = max(t, rounded[step[1]])
        return t

    while any(chains.values()):
        best = None
        for name, chain in chains.items():
            t = begin(chain[0]) if chain else None
            if t is None:
                continue
            engine = stages(chain[0])[0][0]
            stall = max(0.0, t - free[engine])
            if engine != "PE":
                now = t <= free["PE"] and free[engine] <= free["PE"] + SLACK_US
                rank = (0 if now else 3, name == "choose", t)
            else:
                order = {"proj": 2, "logits": 1}.get(name, 0)
                rank = (1, order) if stall <= STALL_US else (2, stall)
            if best is None or rank < best[0]:
                best = (rank, name, t)
        _, name, t = best
        step = chains[name].pop(0)
        place = ring.take(step) if step[0] in AUX_KINDS else None
        for n, (engine, us) in enumerate(stages(step)):
            t = max(t, free[engine]) + us
            free[engine] = t
            if place and step[0] != "back" and (n == 1 or step[0] == "logits"):
                taken[place[:2]] = t
            if step[0] == "mixed":
                taken[backs[step[1:]]] = t
            if step[0] == "proj" and n == 1:
                end[step] = t
            t += 0.1
        end.setdefault(step, t)
        if step[0] == "proj" and step[2]:
            rounded[step[1] + 2] = t + 2.4
        if step[0] == "back":
            backs[step[1:]] = place[:2]
        steps.append(step)
    return steps


STEPS = plan()


def ring_places():
    ring = Ring()
    return {job: ring.take(job) for job in [s for s in STEPS if s[0] in AUX_KINDS] + [("prenorm", 1)]}, ring.begun


AUX, AUX_BEGUN = ring_places()
SQUARES = {s[1]: n for n, s in enumerate([s for s in STEPS if s[0] == "square"])}
LOGITS = {s[1:]: n for n, s in enumerate([s for s in STEPS if s[0] == "logits"])}
GROUPS = {s[1:]: n for n, s in enumerate([s for s in STEPS if s[0] == "scale"])}
GROUP_ORDER = list(GROUPS)
BACKS = {s[1:]: n for n, s in enumerate([s for s in STEPS if s[0] == "back"])}
ROPES = {s[1]: n for n, s in enumerate([s for s in STEPS if s[0] == "rope"])}
NORMS = {s[1]: n for n, s in enumerate([s for s in STEPS if s[0] == "norm"])}
INDEX = {s[1:]: n for n, s in enumerate([s for s in STEPS if s[0] == "index"])}


def turn_of(job):
    return AUX[job][:2]


def hybrid_block(nc, hT, weights, params, consts, out):
    with ExitStack() as ctx:
        def sb(name, shape, dt=F32, scope=ctx):
            return scope.enter_context(nc.sbuf_tensor(name, shape, dt))

        def sem(name):
            return ctx.enter_context(nc.semaphore(name))

        h = sb("h", [128, KT, N])
        xhi = sb("xhi", [128, KT, N], F32R)
        xlo = sb("xlo", [128, KT, N], F32R)
        raw = sb("raw", [128, 2, KT, 128])
        whi = sb("whi", [128, 2, KT, 128], F32R)
        wlo = sb("wlo", [128, 2, KT, 128], F32R)
        cst = sb("cst", [128, N_CST])
        par_all = sb("par_all", [128, DEPTH, N_PAR])
        par = sb("par", [128, N_PAR])
        sqb = sb("sqb", [128, 2, N])
        rnb = sb("rnb", [128, 2, N])
        rstd = sb("rstd", [128, N])
        xnb = sb("xnb", [128, 2, N])
        with ExitStack() as mixers:
            def mb(name, shape, dt=F32):
                return sb(name, shape, dt, mixers)
            with ExitStack() as split_output:
                mix_hi = sb("mix_hi", [128, KT, N], F32R, split_output)
                mix_lo = sb("mix_lo", [128, KT, N], F32R, split_output)
            feat = mb("feat", [128, N_PROJ, N])
            kk = mb("kk", [128, 2, N])
            tok_small = mb("tok_small", [BLK, NB, 128])
            v_fox = mb("v_fox", [BLK, NB, 256])
            v_gla = mb("v_gla", [BLK, NB, 512])
            k_gla = mb("k_gla", [BLK, NB, 256])
            relu = mb("relu", [BLK, 2, N])
            score = mb("score", [BLK, 2, N])
            top8 = mb("top8", [BLK, 8])
            selb = mb("selb", [BLK, 2, N], BF16)
            ident16 = mb("ident16", [BLK, BLK], BF16)
            causal16 = mb("causal16", [BLK, BLK], BF16)
            probs = mb("probs", [BLK, 3, N])
            probs_t = mb("probs_t", [BLK, 2, NB, BLK])
            stat = mb("stat", [BLK, 4, STATS])
            o_tok = mb("o_tok", [BLK, 256])
            c16 = mb("c16", [128, N], BF16)
            sel16 = mb("sel16", [128, 4 * BLK], BF16)
            att = mb("att", [BLK, 2, 2, 2, BLK])
            state = mb("state", [128, 2, 2, 128])
            coef = mb("coef", [128, 2, NB])
        with ExitStack() as ffn:
            hhi = sb("hhi", [128, MF, N], F32R, ffn)
            hlo = sb("hlo", [128, MF, N], F32R, ffn)
            sg = sb("sg", [128, 2, N], F32, ffn)
            hid = sb("hid", [128, 2, N], F32, ffn)
        ps = ctx.enter_context(nc.psum_tensor("ps", [128, 8 * 512], F32))

        par_loaded = sem("par_loaded")
        cst_loaded = sem("cst_loaded")
        h_loaded = [sem(f"h_loaded{k}") for k in range(KT)]
        sq_first = sem("sq_first")
        raw_loaded = [sem("raw_loaded0"), sem("raw_loaded1")]
        hi_done = sem("hi_done")
        split_done = sem("split_done")
        half_done = sem("half_done")
        xhi_ready = sem("xhi_ready")
        x_ready = sem("x_ready")
        layer_open = sem("layer_open")
        h_done = sem("h_done")
        stored = sem("stored")
        par_ready = sem("par_ready")
        masks_ready = sem("masks_ready")
        engines_done = sem("engines_done")
        sq_ready = sem("sq_ready")
        summed = sem("summed")
        rstd_ready = sem("rstd_ready")
        feat_ready = sem("feat_ready")
        job_done = [sem(f"job_done{b}") for b in range(RING)]
        job_taken = [sem(f"job_taken{b}") for b in range(RING)]
        normed = sem("normed")
        roped = sem("roped")
        copied = sem("copied")
        gate_ln = sem("gate_ln")
        fox_ln = sem("fox_ln")
        decay_arg = sem("decay_arg")
        decay_exp = sem("decay_exp")
        decayed = sem("decayed")
        fox_ready = sem("fox_ready")
        fox_part = sem("fox_part")
        c16_ready = sem("c16_ready")
        index_used = sem("index_used")
        selected = sem("selected")
        max_ready = sem("max_ready")
        values_done = sem("values_done")
        heads_ready = sem("heads_ready")
        mixed_hi = sem("mixed_hi")
        rest_done = sem("rest_done")
        state_ready = sem("state_ready")
        sigmoid_ready = sem("sigmoid_ready")
        silu_done = sem("silu_done")
        gla_mixed = sem("gla_mixed")
        gla_hi = sem("gla_hi")
        gla_split = sem("gla_split")
        rn_ready = sem("rn_ready")
        acc_free = sem("acc_free")
        gate_scaled = sem("gate_scaled")
        sg_ready = sem("sg_ready")
        hidden = sem("hidden")
        hhi_ready = sem("hhi_ready")
        hid_ready = sem("hid_ready")
        act_step = sem("act_step")
        dve_step = sem("dve_step")
        layer_sems = range(par_ready.num, dve_step.num + 1)

        def cols(base, n, rows=slice(0, 128)):
            return cst[rows, base:base + n]

        def bank(b, n, rows=slice(0, 128)):
            return ps[rows, b * 512:b * 512 + n]

        def two_banks(b):
            return ps[:, b * 512:(b + 2) * 512].rearrange("p (a c) -> p a c", a=2)[:, :, 0:HALF]

        def halves(ap):
            return ap.rearrange("p (a c) -> p a c", a=2)

        def group_waits():
            last = {}
            for s in BACKS:
                p, n = turn_of(("back",) + s)
                last[p] = max(n, last.get(p, 0))
            return [(job_taken[p], n) for p, n in last.items()]

        def chunks(ap):
            ap = ap[..., 0:NB * BLK]
            return ap.rearrange("p t (c s) -> p t c s" if len(ap.shape) == 3 else "p (c s) -> p c s", s=BLK)

        def block_of(i):
            return slice(i * BLK, (i + 1) * BLK)

        def head_rows(hd):
            return slice(64 * (hd % 2), 64 * (hd % 2) + 64)

        def place(k):
            return PLACES.index(k)

        def pair(k):
            return slice(place(k), place(k) + 2)

        fox_rows = slice(ROW_FF, ROW_FF + 4)

        def part16():
            return xnb[fox_rows, 0].bitcast(BF16)[:, 0:N]

        def fox_gate():
            return feat[fox_rows, place(SMALL)]

        block = ctx.enter_context(nc.Block())

        @block.sync
        def _(sp):
            def load_unit(n, b):
                sp.wait_ge(split_done, n + 1)
                sp.dma_start(raw[:, b].rearrange("p k n -> p (k n)"), weights[n]).then_inc(raw_loaded[b], 16)

            def load_h(k):
                sp.dma_start(h[:, k], hT[k * 128:(k + 1) * 128, :]).then_inc(h_loaded[k], 16)

            load_h(0)
            load_unit(0, 0)
            load_h(2)
            load_unit(1, 1)
            load_h(4)
            sp.dma_start(cst[:], consts).then_inc(cst_loaded, 16)
            with sp.Fori(1, STREAM // 2) as j:
                for b in range(2):
                    load_unit(j * 2 + b, b)
            for k in range(KT):
                sp.wait_ge(h_done, KT * DEPTH + k + 1)
                sp.dma_start(out[k * 128:(k + 1) * 128, :], h[:, k, META:META + SEQ]).then_inc(stored, 16)
            sp.wait_ge(stored, 16 * KT)

        @block.gpsimd
        def _(pool):
            pool.sem_inc(split_done, 2)
            for k in (6, 7):
                pool.dma_start(h[:, k], hT[k * 128:(k + 1) * 128, :]).then_inc(h_loaded[k], 16)
            with pool.Fori(0, STREAM // 2) as j:
                for b in range(2):
                    pool.wait_ge(hi_done, j * 2 + (b + 1))
                    nc.gpsimd.tensor_tensor(wlo[:, b], raw[:, b], whi[:, b].bitcast(F32),
                                            ALU.subtract).then_inc(split_done, 1)

        @block.tensor
        def _(pe):
            pe.sem_inc(half_done, 4)
            with pe.Fori(0, DEPTH) as l:
                ident, ones = cols(C_ID, 128), cols(C_ONE, 128)

                def job_begin(job):
                    p, _, before = AUX[job]
                    for q, n in before:
                        pe.wait_ge(job_taken[q], n)
                    return 4 + p, job_done[p]

                def wait_taken(job):
                    p, n = turn_of(job)
                    pe.wait_ge(job_taken[p], n)

                def unit_half(b, n, bank_no, hf, x, order=range(KT), first=True, last=True, waits={}):
                    if hf == 0:
                        pe.wait_ge(hi_done, l * UNITS + (n + 1))
                    cut = slice(hf * HALF, (hf + 1) * HALF)
                    for k in order:
                        for w in waits.get(k, ()):
                            pe.wait_ge(*w)
                        for t in range(2):
                            nc.tensor.matmul(bank(bank_no, HALF), whi[:, b, k % KT], x(k)[t][:, cut],
                                             start=(first and k == order[0] and t == 0), stop=False)
                    if hf == 0:
                        pe.wait_ge(split_done, l * UNITS + (n + 3))
                    for k in order:
                        ins = nc.tensor.matmul(bank(bank_no, HALF), wlo[:, b, k % KT], x(k)[0][:, cut], start=False,
                                               stop=(last and k == order[-1]))
                    ins.then_inc(half_done, 1)

                def x_tiles(k):
                    return xhi[:, k], xlo[:, k]

                def mix_tiles(k):
                    return mix_hi[:, k], mix_lo[:, k]

                def prenorm(s):
                    b0, done = job_begin(("prenorm", s))
                    if s == 0:
                        pe.wait_ge(cst_loaded, 16)
                        pe.wait_ge(h_done, l * KT + KT)
                    else:
                        pe.wait_ge(summed, KT)
                    for hf in range(2):
                        ins = nc.tensor.matmul(bank(b0 + hf, HALF), ones, rstd[:, hf * HALF:(hf + 1) * HALF],
                                               start=True, stop=True)
                    ins.then_inc(done, 1)

                def proj(k, hf):
                    q = 2 * k + hf
                    if q >= 3:
                        pe.wait_ge(feat_ready, q - 2)
                    unit_half(k % 2, k, q % 3, hf, x_tiles,
                              waits={n: [(x_ready, l * (2 * KT) + (n + 1))] for n in range(KT)} if q == 0 else {})

                def norm(k):
                    b0, done = job_begin(("norm", k))
                    pe.wait_ge(sq_ready, SQUARES[k] + 1)
                    lhs = cols(C_BLK, 128) if k < GV else ones
                    for hf in range(2):
                        ins = nc.tensor.matmul(bank(b0 + hf, HALF), lhs,
                                               sqb[:, SQUARES[k] % 2, hf * HALF:(hf + 1) * HALF], start=True, stop=True)
                    ins.then_inc(done, 1)

                def rope(k):
                    b0, done = job_begin(("rope", k))
                    if k in NORMS:
                        pe.wait_ge(normed, NORMS[k] + 1)
                    pe.wait_ge(feat_ready, 2 * k + 2)
                    for hf in range(2):
                        ins = nc.tensor.matmul(bank(b0 + hf, HALF), cols(C_ROT, 128),
                                               feat[:, place(k), hf * HALF:(hf + 1) * HALF], start=True, stop=True)
                    ins.then_inc(done, 1)

                def turn_tile(k):
                    b0, done = job_begin(("turn_tile", k))
                    pe.wait_ge(feat_ready, 2 * k + 2)
                    turn_blocks(feat[:, place(k), :], b0, done)

                def turn_k(t):
                    b0, done = job_begin(("turn_k", t))
                    pe.wait_ge(decayed, 2)
                    turn_blocks(feat[:, place(GK + t), :], b0, done)

                def turn_blocks(src, b0, done):
                    for i in range(NB):
                        col = b0 * 512 + i * 128
                        ins = nc.tensor.transpose(ps[0:BLK, col:col + 128], src[:, block_of(i)], ident)
                    ins.then_inc(done, 1)

                def gate(t):
                    b0, done = job_begin(("gate", t))
                    pe.wait_ge(feat_ready, 2 * SMALL + 2)
                    rows = slice(ROW_LR, ROW_LR + RANK)
                    for hf in range(2):
                        ins = nc.tensor.matmul(bank(b0 + hf, HALF), par[rows, P_W2 + t * 128:P_W2 + (t + 1) * 128],
                                               feat[rows, place(SMALL), hf * HALF:(hf + 1) * HALF], start=True, stop=True)
                    ins.then_inc(done, 1)

                def pieces(n):
                    return [(0, min(n, 512))] + ([(512, n)] if n > 512 else [])

                def index(i, hd):
                    b0, done = job_begin(("index", i, hd))
                    if (i, hd) == (1, 0):
                        pe.wait_ge(roped, len(ROPES))
                        pe.wait_ge(copied, 2)
                    r = head_rows(hd)
                    for a, z in pieces((i + 1) * BLK):
                        ins = nc.tensor.matmul(ps[0:BLK, b0 * 512 + a:b0 * 512 + z], feat[r, place(IQ + hd // 2), block_of(i)],
                                               kk[r, 1, a:z], start=True, stop=True)
                    ins.then_inc(done, 1)

                def logits(g, i, hd):
                    b0, done = job_begin(("logits", g, i, hd))
                    if LOGITS[(g, i, hd)] == 0:
                        pe.wait_ge(masks_ready, 5)
                    r = head_rows(hd)
                    n = (i + 1) * BLK
                    if g == 0:
                        q, key = feat[r, place(DQ + hd // 2), block_of(i)], kk[r, 0, :]
                        if hd == 0:
                            pe.wait_ge(roped, len(ROPES))
                            pe.wait_ge(copied, 2)
                            if i:
                                pe.wait_ge(selected, i)
                    else:
                        q, key = feat[r, place(FQ + hd // 2), block_of(i)], feat[r, place(FK + hd // 2), :]
                        if hd == 0:
                            pe.wait_ge(normed, NORMS[FK + 1] + 1)
                            pe.wait_ge(c16_ready, 3)
                    for a, z in pieces(n):
                        o = ps[0:BLK, b0 * 512 + a:b0 * 512 + z]
                        last = z == n and g == 0 and i > 0
                        ins = nc.tensor.matmul(o, q, key[:, a:z], start=True, stop=False)
                        if g == 1:
                            ins = nc.tensor.matmul(o, sel16[:, hd * BLK:(hd + 1) * BLK], c16[:, a:z],
                                                   start=False, stop=(z <= i * BLK))
                        if g == 0 and i > 0:
                            ins = nc.tensor.matmul(o, ident16[:], selb[:, i % 2, a:z], start=False, stop=True)
                        else:
                            lo = max(a, i * BLK)
                            if z > lo:
                                ins = nc.tensor.matmul(ps[0:BLK, b0 * 512 + lo:b0 * 512 + z], ident16[:],
                                                       causal16[:, lo - i * BLK:z - i * BLK], start=False, stop=True)
                    ins.then_inc(done, 1)

                def turn(g, i, hd):
                    b0, done = job_begin(("turn", g, i, hd))
                    wait_taken(("logits", g, i, hd))
                    u = LOGITS[(g, i, hd)]
                    for j in range(i + 1):
                        col = b0 * 512 + j * 128
                        ins = nc.tensor.transpose(ps[0:BLK, col:col + BLK], probs[:, u % 3, block_of(j)],
                                                  cols(C_ID, BLK, slice(0, BLK)))
                    ins.then_inc(done, 1)

                def values(g, i, hd):
                    wait_taken(("turn", g, i, hd))
                    u, grp = LOGITS[(g, i, hd)], GROUPS[(g, i)]
                    if hd == 0:
                        if grp:
                            pe.wait_ge(heads_ready, grp)
                        for t in ((SMALL,) if g == 0 else (FV, FV + 1)):
                            wait_taken(("turn_tile", t))
                    for j in range(i + 1):
                        v = tok_small[:, j, 0:64] if g == 0 else v_fox[:, j, hd * 64:(hd + 1) * 64]
                        ins = nc.tensor.matmul(ps[0:BLK, 3 * 512 + hd * 64:3 * 512 + (hd + 1) * 64],
                                               probs_t[:, u % 2, j, :], v, start=(j == 0), stop=(j == i))
                    ins.then_inc(values_done, 1)

                def back(g, i):
                    b0, done = job_begin(("back", g, i))
                    pe.wait_ge(heads_ready, GROUPS[(g, i)] + 1)
                    for t in range(2):
                        ins = nc.tensor.transpose(ps[:, b0 * 512 + t * BLK:b0 * 512 + (t + 1) * BLK],
                                                  o_tok[:, t * 128:(t + 1) * 128], cols(C_ID, BLK, slice(0, BLK)))
                    ins.then_inc(done, 1)

                def gla_place(b0, hd):
                    col = (b0 + hd % 2) * 512 + (hd // 2) * BLK
                    return ps[:, col:col + BLK]

                def gla_att(c):
                    b0, done = job_begin(("gla_att", c))
                    pe.wait_ge(decayed, 2)
                    for hd in range(4):
                        r = head_rows(hd)
                        ins = nc.tensor.matmul(gla_place(b0, hd)[0:BLK],
                                               feat[r, place(GK + hd // 2), block_of(c)], feat[r, place(GQ + hd // 2), block_of(c)],
                                               start=True, stop=True)
                    ins.then_inc(done, 1)

                def gla_out(c):
                    b0, done = job_begin(("gla_out", c))
                    wait_taken(("gla_att", c))
                    if c == 0:
                        for t in range(4):
                            wait_taken(("turn_tile", GV + t))
                    else:
                        pe.wait_ge(state_ready, c)
                    for hd in range(4):
                        r = head_rows(hd)
                        o = gla_place(b0, hd)
                        if c:
                            nc.tensor.matmul(o, state[r, (c - 1) % 2, hd // 2, :], feat[r, place(GQ + hd // 2), block_of(c)],
                                             start=True, stop=False)
                        ins = nc.tensor.matmul(o, v_gla[:, c, hd * 128:(hd + 1) * 128], att[:, c % 2, hd % 2, hd // 2, :],
                                               start=(c == 0), stop=True)
                    ins.then_inc(done, 1)

                def gla_kv(c):
                    b0, done = job_begin(("gla_kv", c))
                    if c == 0:
                        for t in range(2):
                            wait_taken(("turn_k", t))
                    for t in range(2):
                        ins = nc.tensor.matmul(ps[:, b0 * 512 + t * 256:b0 * 512 + (t + 1) * 256],
                                               k_gla[:, c, t * 128:(t + 1) * 128], v_gla[:, c, t * 256:(t + 1) * 256],
                                               start=True, stop=True)
                    ins.then_inc(done, 1)

                do = dict(prenorm=prenorm, proj=proj, norm=norm, rope=rope, turn_tile=turn_tile, turn_k=turn_k, gate=gate,
                          index=index, logits=logits, turn=turn, values=values, back=back, gla_att=gla_att,
                          gla_out=gla_out, gla_kv=gla_kv)
                for step in STEPS:
                    if step[0] in do:
                        do[step[0]](*step[1:])

                pe.wait_ge(feat_ready, 2 * N_PROJ)
                with pe.Fori(0, N_OUT // 2) as j:
                    for b in range(2):
                        pe.wait_ge(acc_free, j * 2 + (b + 1))
                        for hf in range(2):
                            unit_half(b, j * 2 + (U_OUT + b), 2 * b + hf, hf, mix_tiles, order=(4, 5, 6, 7, 0, 1, 2, 3),
                                      waits={4: [(gla_split, 4)], 0: group_waits() + [(rest_done, 4)]} if hf == 0 else {})

                def gate_up(j, b, begin=False):
                    pe.wait_ge(acc_free, j * 2 + (N_OUT + b + 1))
                    for s in range(2):
                        for hf in range(2):
                            unit_half(s, j * 4 + (U_GU + 2 * b + s), 4 * b + 2 * s + hf, hf, x_tiles,
                                      waits={n: [(x_ready, l * (2 * KT) + (KT + n + 1))] for n in range(KT)} if begin and s == hf == 0 else {})
                        if begin and s == 0:
                            prenorm(1)

                gate_up(0, 0, begin=True)
                for q in range(RING):
                    pe.wait_ge(job_taken[q], AUX_BEGUN[q])
                gate_up(0, 1)
                with pe.Fori(1, MF // 2) as j:
                    for b in range(2):
                        gate_up(j, b)
                with pe.Fori(0, KT // 2) as j:
                    for b in range(2):
                        pe.wait_ge(acc_free, j * 2 + (N_OUT + MF + b + 1))
                        for s, kts in enumerate(DN_PARTS):
                            k0 = sum(DN_PARTS[:s])
                            for hf in range(2):
                                unit_half((3 * b + s) % 2, j * 6 + (U_DN + 3 * b + s), 2 * b + hf, hf, lambda k: (hhi[:, k], hlo[:, k]),
                                          order=range(k0, k0 + kts), first=(s == 0), last=(s == 2),
                                          waits={k0: [(hid_ready, k0 + kts)]} if hf == 0 else {})
                pe.drain().then_inc(engines_done, 1)
                pe.wait_ge(layer_open, l + 1)

        @block.scalar
        def _(act):
            act.dma_start(par_all[:], params.rearrange("l p n -> p l n")).then_inc(par_loaded, 16)
            for k in (1, 3, 5):
                act.dma_start(h[:, k], hT[k * 128:(k + 1) * 128, :]).then_inc(h_loaded[k], 16)
            nc.scalar.preload_act_table_set("natural_log_exp_and_others")
            eps = cols(C_EPS, 1)

            def x_high(k, gain):
                nc.scalar.activation(xhi[:, k], h[:, k], ACT.Copy, scale=gain).then_inc(xhi_ready, 1)

            def square_of(k, slot):
                return nc.scalar.activation(sqb[:, slot], h[:, k], ACT.Square)

            def round_slot(b):
                return nc.scalar.activation(whi[:, b], raw[:, b], ACT.Copy).then_inc(hi_done, 1)

            act.wait_ge(par_loaded, 16)
            for k in range(KT):
                act.wait_ge(h_loaded[k], 16)
                x_high(k, par_all[:, 0, P_ATT + k:P_ATT + k + 1])
                if k in (0, 5):
                    act.wait_ge(raw_loaded[k // 5], 16)
                    round_slot(k // 5)
            for k in range(KT):
                if k >= 2:
                    act.wait_ge(h_done, k - 1)
                square_of(k, k % 2).then_inc(sq_first, 1)
            with act.Fori(0, DEPTH) as l:
                half0 = act.snap(l * (2 * UNITS) + 4)
                raw0 = act.snap(l * (8 * UNITS))
                own = [0]

                def round_unit(n, slot):
                    act.wait_ge(half_done, half0 + (n * 2 - 2))
                    act.wait_ge(raw_loaded[slot], raw0 + (n - slot) * 8 + 16)
                    round_slot(slot)

                def chain(ins):
                    own[0] += 1
                    ins.then_inc(act_step, 1)
                    act.wait_ge(act_step, own[0])

                def wait_done(job):
                    p, n = turn_of(job)
                    act.wait_ge(job_done[p], n)
                    return 4 + p, job_taken[p], n

                def rsqrt_mean(job, count, dst):
                    b0, taken, n = wait_done(job)
                    nc.scalar.activation(halves(dst), two_banks(b0), ACT.Ln, bias=eps, scale=1.0 / count).then_inc(taken, 1)
                    act.wait_ge(taken, n)

                def prenorm(s):
                    act.wait_ge(cst_loaded, 16)
                    rsqrt_mean(("prenorm", s), D, rstd[:])
                    nc.scalar.activation(rstd[:], rstd[:], ACT.Exp, scale=-0.5).then_inc(rstd_ready, 1)

                def proj(k, hf):
                    if hf == 1:
                        round_unit(k + 2, k % 2)

                def square(k):
                    n = SQUARES[k]
                    if k < GV:
                        act.wait_ge(feat_ready, 2 * k + 2)
                    else:
                        p, m = turn_of(("gla_out", NB - 1))
                        act.wait_ge(job_taken[p], m)
                    if n >= 2:
                        before = [s for s in STEPS if s[0] == "square"][n - 2][1]
                        wait_done(("norm", before))
                    nc.scalar.activation(sqb[:, n % 2], feat[:, place(k)], ACT.Square).then_inc(sq_ready, 1)

                def norm(k):
                    n = NORMS[k]
                    if n >= 2:
                        act.wait_ge(normed, n - 1)
                    dst = rnb[:, n % 2]
                    rsqrt_mean(("norm", k), 64 if k < GV else 128, dst)
                    nc.scalar.activation(dst, dst, ACT.Exp, scale=-0.5).then_inc(rn_ready, 1)

                def copies():
                    act.wait_ge(roped, ROPES[2] + 1)
                    nc.scalar.activation(kk[64:128, 0], kk[0:64, 0], ACT.Copy).then_inc(copied, 1)
                    nc.scalar.activation(kk[0:64, 1], kk[64:128, 1], ACT.Copy).then_inc(copied, 1)

                def take_blocks(job, dst):
                    b0, taken, _ = wait_done(job)
                    nc.scalar.activation(dst, ps[0:BLK, b0 * 512:b0 * 512 + NB * 128].rearrange("p (i c) -> p i c", i=NB),
                                         ACT.Copy).then_inc(taken, 1)

                def turn_tile(k):
                    take_blocks(("turn_tile", k),
                                tok_small[:] if k == SMALL else
                                v_fox[:, :, (k - FV) * 128:(k - FV + 1) * 128] if k < GV else
                                v_gla[:, :, (k - GV) * 128:(k - GV + 1) * 128])

                def turn_k(t):
                    take_blocks(("turn_k", t), k_gla[:, :, t * 128:(t + 1) * 128])

                def gate(t):
                    b0, taken, _ = wait_done(("gate", t))
                    nc.scalar.activation(halves(feat[:, place(GG + 2 + t)]), two_banks(b0), ACT.Identity,
                                         bias=par[:, P_GB + t:P_GB + t + 1]).then_inc(taken, 1)

                def gate_log():
                    for t in range(2):
                        p, n = turn_of(("gate", t))
                        act.wait_ge(job_taken[p], n)
                    e = feat[:, pair(GG)]
                    chain(nc.scalar.activation(e, feat[:, pair(GG + 2)], ACT.Abs))
                    chain(nc.scalar.activation(e, e, ACT.Exp, scale=-1.0))
                    nc.scalar.activation(e, e, ACT.Ln, bias=cols(C_ONE, 1)).then_inc(gate_ln, 1)

                def gate_exp():
                    act.wait_ge(decay_arg, 1)
                    nc.scalar.activation(coef[:, :, 0:NB - 1], coef[:, :, 0:NB - 1], ACT.Exp, scale=1.0 / TAU).then_inc(decay_exp, 1)
                    act.wait_ge(decay_arg, 2)
                    e, d = feat[:, pair(GG)], feat[:, pair(GG + 2)]
                    chain(nc.scalar.activation(e, d, ACT.Exp, scale=1.0 / TAU))
                    nc.scalar.activation(d, d, ACT.Exp, scale=-1.0 / TAU).then_inc(decay_exp, 1)

                def fox_log():
                    p, n = turn_of(("turn_tile", SMALL))
                    act.wait_ge(job_done[p], n)
                    act.wait_ge(feat_ready, 2 * SMALL + 2)
                    chain(nc.scalar.activation(fox_gate(), fox_gate(), ACT.Identity, bias=par[fox_rows, P_FB:P_FB + 1]))
                    act.wait_ge(roped, len(ROPES))
                    f = xnb[fox_rows, 0]
                    chain(nc.scalar.activation(f, fox_gate(), ACT.Abs))
                    chain(nc.scalar.activation(f, f, ACT.Exp, scale=-1.0))
                    nc.scalar.activation(f, f, ACT.Ln, bias=cols(C_ONE, 1, fox_rows)).then_inc(fox_ln, 1)

                def fox_parts():
                    act.wait_ge(fox_part, 1)
                    nc.scalar.activation(c16[64:68], part16(), ACT.Copy).then_inc(c16_ready, 1)
                    act.wait_ge(fox_part, 2)
                    nc.scalar.activation(c16[32:36], fox_gate(), ACT.Copy).then_inc(c16_ready, 1)

                def index(i, hd):
                    b0, taken, _ = wait_done(("index", i, hd))
                    n = INDEX[(i, hd)]
                    if n >= 2:
                        act.wait_ge(index_used, n - 1)
                    nk = (i + 1) * BLK
                    nc.scalar.activation(relu[:, n % 2, 0:nk], ps[0:BLK, b0 * 512:b0 * 512 + nk], ACT.Relu,
                                         scale=1.0 / 16).then_inc(taken, 1)

                def logits(g, i, hd):
                    b0, taken, _ = wait_done(("logits", g, i, hd))
                    u = LOGITS[(g, i, hd)]
                    w = u % STATS
                    act.wait_ge(max_ready, 2 * u + 2)
                    if u >= 3:
                        before = [s for s in STEPS if s[0] == "logits"][u - 3][1:]
                        wait_done(("turn",) + before)
                    nk = (i + 1) * BLK
                    nc.scalar.activation(probs[:, u % 3, 0:nk], ps[0:BLK, b0 * 512:b0 * 512 + nk], ACT.Exp,
                                         bias=stat[:, 1, w:w + 1], scale=0.125,
                                         accum_out=stat[:, 2, w:w + 1]).then_inc(taken, 1)

                def turn(g, i, hd):
                    b0, taken, _ = wait_done(("turn", g, i, hd))
                    u = LOGITS[(g, i, hd)]
                    if u >= 2:
                        act.wait_ge(values_done, u - 1)
                    nc.scalar.activation(probs_t[:, u % 2, 0:i + 1], ps[0:BLK, b0 * 512:b0 * 512 + (i + 1) * 128]
                                         .rearrange("p (j q) -> p j q", q=128)[:, :, 0:BLK], ACT.Copy).then_inc(taken, 1)

                def gla_out(c):
                    b0, taken, _ = wait_done(("gla_out", c))
                    for a in range(2):
                        ins = nc.scalar.activation(feat[:, place(GV + a):place(GV + a) + 3:2, block_of(c)], bank(b0 + a, 2 * BLK)
                                                   .rearrange("p (h t) -> p h t", h=2), ACT.Copy)
                    ins.then_inc(taken, 1)

                def silu(hd):
                    act.wait_ge(feat_ready, 2 * (GG + hd) + 2)
                    if hd >= 2:
                        act.wait_ge(silu_done, hd - 1)
                    else:
                        act.wait_ge(c16_ready, 3)
                        act.wait_ge(roped, len(ROPES))
                    s = xnb[:, hd % 2]
                    chain(nc.scalar.activation(s, feat[:, place(GG + hd)], ACT.Exp, scale=-1.0))
                    chain(nc.scalar.activation(s, s, ACT.Ln, bias=cols(C_ONE, 1)))
                    nc.scalar.activation(s, s, ACT.Exp, scale=-1.0).then_inc(sigmoid_ready, 1)

                def mixed(g, i):
                    b0, _, _ = wait_done(("back", g, i))
                    if g:
                        act.wait_ge(c16_ready, 3)
                    nc.scalar.activation(mix_hi[:, 2 * g:2 * g + 2, block_of(i)],
                                         bank(b0, 2 * BLK).rearrange("p (t q) -> p t q", t=2), ACT.Copy).then_inc(mixed_hi, 1)

                def gla_mix(hd):
                    act.wait_ge(gla_mixed, hd + 1)
                    nc.scalar.activation(mix_hi[:, 4 + hd], feat[:, place(GG + hd)], ACT.Copy).then_inc(gla_hi, 1)

                act.wait_ge(par_ready, 1)
                do = dict(prenorm=prenorm, proj=proj, square=square, norm=norm, copies=copies, turn_tile=turn_tile,
                          turn_k=turn_k, gate=gate, gate_log=gate_log, gate_exp=gate_exp, fox_log=fox_log, fox_parts=fox_parts,
                          index=index, logits=logits, turn=turn, mixed=mixed,
                          gla_out=gla_out, silu=silu, gla_mix=gla_mix)
                for step in STEPS:
                    if step[0] in do:
                        do[step[0]](*step[1:])

                for m in range(KT):
                    round_unit(U_OUT + m + 2, m % 2)
                    act.wait_ge(acc_free, 2 + m + 1)
                    x_high(m, par[:, P_FFN + m:P_FFN + m + 1])
                    if m >= 2:
                        act.wait_ge(summed, m - 1)
                    else:
                        wait_done(("norm", GV + 3))
                    square_of(m, m % 2).then_inc(sq_ready, 1)
                prenorm(1)
                nc.scalar.preload_act_table_set("silu_and_others")
                with act.Fori(0, MF // 2) as j:
                    for b in range(2):
                        round_unit(j * 4 + (U_GU + 2 * b + 2), 0)
                        act.wait_ge(gate_scaled, j * 2 + (b + 1))
                        nc.scalar.activation(sg[:, b], sg[:, b], ACT.Silu).then_inc(sg_ready, 1)
                        round_unit(j * 4 + (U_GU + 2 * b + 3), 1)
                        act.wait_ge(hidden, j * 2 + (b + 1))
                        nc.scalar.activation(hhi[:, bass.ds(j * 2 + b, 1), :].rearrange("p a t -> p (a t)"),
                                             hid[:, b], ACT.Copy).then_inc(hhi_ready, 1)

                nc.scalar.preload_act_table_set("natural_log_exp_and_others")

                for m in range(KT):
                    for s in range(3):
                        round_unit(U_DN + 3 * m + s + 2, (3 * m + s) % 2)
                    act.wait_ge(acc_free, 2 + N_OUT + MF + m + 1)
                    x_high(m, par[:, P_NEXT + m:P_NEXT + m + 1])
                    act.wait_ge(h_done, l * KT + (KT + m - 1))
                    square_of(m, m % 2).then_inc(sq_ready, 1)
                act.drain().then_inc(engines_done, 1)
                act.wait_ge(layer_open, l + 1)

        @block.vector
        def _(dve):
            def x_low(k, gain, n):
                dve.wait_ge(xhi_ready, n + 1)
                nc.vector.scalar_tensor_tensor(xlo[:, k], h[:, k], gain, xhi[:, k].bitcast(F32), ALU.mult,
                                               ALU.subtract).then_inc(x_ready, 1)

            dve.wait_ge(par_loaded, 16)
            for k in range(KT):
                x_low(k, par_all[:, 0, P_ATT + k:P_ATT + k + 1], k)
            for k in range(KT):
                dve.wait_ge(sq_first, k + 1)
                if k:
                    dve.wait_ge(h_done, k)
                    nc.vector.tensor_tensor(rstd[:], rstd[:], sqb[:, k % 2], ALU.add).then_inc(h_done, 1)
                else:
                    nc.vector.tensor_copy(rstd[:], sqb[:, 0]).then_inc(h_done, 1)
            with dve.Fori(0, DEPTH) as l:
                half0 = dve.snap(l * (2 * UNITS) + 4)
                own = [0]

                def chain(ins):
                    own[0] += 1
                    ins.then_inc(dve_step, 1)
                    dve.wait_ge(dve_step, own[0])

                nc.vector.tensor_copy(par[:], par_all[:, bass.ds(l, 1), :].rearrange("p a n -> p (a n)")).then_inc(par_ready, 1)
                dve.wait_ge(par_ready, 1)
                dve.sem_inc(acc_free, 2)

                def wait_done(job):
                    p, n = turn_of(job)
                    dve.wait_ge(job_done[p], n)
                    return 4 + p, job_taken[p], n

                def proj(k, hf):
                    if (k, hf) == (0, 0):
                        dve.wait_ge(rstd_ready, 1)
                    if (k, hf) == (1, 0):
                        dve.wait_ge(cst_loaded, 16)
                        nc.vector.tensor_copy(ident16[:], cols(C_ID, BLK, slice(0, BLK))).then_inc(masks_ready, 1)
                        nc.vector.tensor_copy(causal16[:], cols(C_CAU, BLK, slice(0, BLK))).then_inc(masks_ready, 1)
                        nc.vector.memset(att[:].rearrange("p c a h t -> p (c a h t)"), 0.0).then_inc(masks_ready, 1)
                        nc.vector.memset(c16[:], 0.0).then_inc(masks_ready, 1)
                        nc.vector.tensor_copy(sel16[:].rearrange("p (h q) -> p h q", h=4), cols(C_SEL, 4)
                                              .rearrange("p (h a) -> p h a", a=1).broadcast_to([128, 4, BLK])).then_inc(masks_ready, 1)
                        dve.wait_ge(masks_ready, 5)
                    if k == GG and hf == 0:
                        dve.wait_ge(decayed, 2)
                    dve.wait_ge(half_done, half0 + (2 * k + hf + 1))
                    cut = slice(hf * HALF, (hf + 1) * HALF)
                    nc.vector.tensor_tensor(feat[:, place(k), cut], bank((2 * k + hf) % 3, HALF), rstd[:, cut],
                                            ALU.mult).then_inc(feat_ready, 1)

                def norm(k):
                    n = NORMS[k]
                    dve.wait_ge(rn_ready, n + 1)
                    dve.wait_ge(feat_ready, 2 * k + 2)
                    if k < GV:
                        rows = slice(0, 64) if k == DKIK else slice(0, 128)
                        g = NORMED[k]
                        nc.vector.scalar_tensor_tensor(feat[rows, place(k)], feat[rows, place(k)], par[rows, g:g + 1], rnb[rows, n % 2],
                                                       ALU.mult, ALU.mult).then_inc(normed, 1)
                    else:
                        nc.vector.scalar_tensor_tensor(feat[:, place(k)], feat[:, place(k)], par[:, P_GO:P_GO + 1], rnb[:, n % 2],
                                                       ALU.mult, ALU.mult).then_inc(normed, 1)
                    dve.wait_ge(normed, n + 1)

                def rope(k):
                    b0, taken, n = wait_done(("rope", k))
                    dve.wait_ge(feat_ready, 2 * k + 2)
                    chain(nc.vector.tensor_tensor(xnb[:, 0], feat[:, place(k)], cols(C_COS, N), ALU.mult))
                    nc.vector.tensor_tensor(halves(xnb[:, 1]), two_banks(b0), halves(cols(C_SIN, N)), ALU.mult).then_inc(taken, 1)
                    dve.wait_ge(taken, n)
                    if k == DKIK:
                        chain(nc.vector.tensor_tensor(kk[0:64, 0], xnb[0:64, 0], xnb[0:64, 1], ALU.add))
                        nc.vector.tensor_tensor(kk[64:128, 1], xnb[64:128, 0], xnb[64:128, 1], ALU.add).then_inc(roped, 1)
                    else:
                        nc.vector.tensor_tensor(feat[:, place(k)], xnb[:, 0], xnb[:, 1], ALU.add).then_inc(roped, 1)
                    dve.wait_ge(roped, ROPES[k] + 1)

                def gate_log():
                    e, z = feat[:, pair(GG)], feat[:, pair(GG + 2)]
                    dve.wait_ge(gate_ln, 1)
                    chain(nc.vector.scalar_tensor_tensor(z, z, 0.0, e, ALU.min, ALU.subtract))
                    for t in range(2):
                        chain(nc.vector.tensor_tensor_scan(feat[:, place(GG + t)], cols(C_RST, N), feat[:, place(GG + 2 + t)], 0.0,
                                                           ALU.mult, ALU.add))
                    b = chunks(e)
                    mid, end = b[:, :, :, BLK // 2 - 1], b[:, :, :, BLK - 1]
                    chain(nc.vector.tensor_tensor(coef[:, :, 0:NB - 1], end[:, :, 0:NB - 1], mid[:, :, 0:NB - 1], ALU.subtract))
                    nc.vector.tensor_tensor(coef[:, :, 0:NB - 1], coef[:, :, 0:NB - 1], mid[:, :, 1:NB], ALU.add).then_inc(decay_arg, 1)
                    for t in range(2):
                        centre = chunks(feat[:, place(GG + t)])[:, :, BLK // 2 - 1:BLK // 2]
                        ins = nc.vector.tensor_tensor(chunks(feat[:, place(GG + 2 + t)]),
                                                      chunks(feat[:, place(GG + t)]),
                                                      centre.broadcast_to([128, NB, BLK]), ALU.subtract)
                        if t == 0:
                            chain(ins)
                    ins.then_inc(decay_arg, 1)

                def fox_log():
                    dve.wait_ge(fox_ln, 1)
                    chain(nc.vector.scalar_tensor_tensor(xnb[fox_rows, 1], fox_gate(), 0.0, xnb[fox_rows, 0], ALU.min,
                                                         ALU.subtract))
                    nc.vector.tensor_tensor_scan(fox_gate(), cst[fox_rows, C_COS:C_COS + N], xnb[fox_rows, 1], 0.0,
                                                 ALU.mult, ALU.add).then_inc(fox_ready, 1)
                    dve.wait_ge(fox_ready, 1)
                    nc.vector.tensor_copy(c16[fox_rows], fox_gate()).then_inc(c16_ready, 1)
                    dve.wait_ge(c16_ready, 1)
                    chain(nc.vector.tensor_tensor(fox_gate(), fox_gate(), c16[fox_rows], ALU.subtract))
                    nc.vector.tensor_copy(part16(), fox_gate()).then_inc(fox_part, 1)
                    dve.wait_ge(fox_part, 1)
                    nc.vector.tensor_tensor(fox_gate(), fox_gate(), part16(), ALU.subtract).then_inc(fox_part, 1)

                def decays():
                    dve.wait_ge(decay_exp, 2)
                    dve.wait_ge(feat_ready, 2 * (GK + 1) + 2)
                    nc.vector.scalar_tensor_tensor(feat[:, pair(GQ)], feat[:, pair(GQ)], 0.125, feat[:, pair(GG)],
                                                   ALU.mult, ALU.mult).then_inc(decayed, 1)
                    nc.vector.tensor_tensor(feat[:, pair(GK)], feat[:, pair(GK)], feat[:, pair(GG + 2)],
                                            ALU.mult).then_inc(decayed, 1)

                def index(i, hd):
                    n = INDEX[(i, hd)]
                    nk = (i + 1) * BLK
                    p, m = turn_of(("index", i, hd))
                    dve.wait_ge(job_taken[p], m)
                    if n == 0:
                        p, m = turn_of(("turn_tile", SMALL))
                        dve.wait_ge(job_taken[p], m)
                    w = tok_small[:, i, ROW_IW + hd:ROW_IW + hd + 1]
                    if hd == 0:
                        ins = nc.vector.tensor_scalar(score[:, i % 2, 0:nk], relu[:, n % 2, 0:nk], w, None, ALU.mult)
                    else:
                        ins = nc.vector.scalar_tensor_tensor(score[:, i % 2, 0:nk], relu[:, n % 2, 0:nk], w, score[:, i % 2, 0:nk],
                                                             ALU.mult, ALU.add)
                    ins.then_inc(index_used, 1)
                    dve.wait_ge(index_used, n + 1)
                    if hd == 3:
                        chain(nc.vector.tensor_tensor(score[:, i % 2, block_of(i)], score[:, i % 2, block_of(i)],
                                                      cols(C_CAU, BLK, slice(0, BLK)), ALU.add))

                def topk(i, r0):
                    nk = (i + 1) * BLK
                    for _ in range(TOPK_ROUNDS):
                        chain(nc.vector.max(top8[:], score[:, i % 2, 0:nk]))
                        chain(nc.vector.match_replace(out=score[:, i % 2, 0:nk], in_to_replace=top8[:],
                                                      in_values=score[:, i % 2, 0:nk], imm_value=TAKEN))

                def select(i):
                    nk = (i + 1) * BLK
                    if i >= 3:
                        wait_done(("logits", 0, i - 2, 3))
                    chain(nc.vector.tensor_scalar(selb[:, i % 2, 0:nk], score[:, i % 2, 0:nk], TAKEN / 2, NEG, ALU.is_gt, ALU.mult))
                    nc.vector.tensor_tensor(selb[:, i % 2, block_of(i)], selb[:, i % 2, block_of(i)], causal16[:],
                                            ALU.add).then_inc(selected, 1)
                    dve.wait_ge(selected, i)

                def logits(g, i, hd):
                    b0, taken, _ = wait_done(("logits", g, i, hd))
                    u = LOGITS[(g, i, hd)]
                    w = u % STATS
                    nk = (i + 1) * BLK
                    nc.vector.reduce_max(stat[:, 0, w:w + 1], ps[0:BLK, b0 * 512:b0 * 512 + nk], AX.X).then_inc(max_ready, 1)
                    dve.wait_ge(max_ready, 2 * u + 1)
                    nc.vector.tensor_scalar_mul(stat[:, 1, w:w + 1], stat[:, 0, w:w + 1], -0.125).then_inc(max_ready, 1)

                def scale(g, i):
                    u, grp = LOGITS[(g, i, 3)], GROUPS[(g, i)]
                    w = (u - 3) % STATS
                    p, n = turn_of(("logits", g, i, 3))
                    dve.wait_ge(job_taken[p], n)
                    if grp:
                        wait_done(("back",) + GROUP_ORDER[grp - 1])
                    chain(nc.vector.reciprocal(stat[:, 3, w:w + 4], stat[:, 2, w:w + 4]))
                    dve.wait_ge(values_done, u + 1)
                    nc.vector.tensor_tensor(o_tok[:].rearrange("p (h d) -> p h d", h=4),
                                            ps[0:BLK, 3 * 512:3 * 512 + 256].rearrange("p (h d) -> p h d", h=4),
                                            stat[:, 3, w:w + 4].rearrange("p (h a) -> p h a", a=1)
                                            .broadcast_to([BLK, 4, 64]), ALU.mult).then_inc(heads_ready, 1)

                def mixed(g, i):
                    dve.wait_ge(mixed_hi, BACKS[(g, i)] + 1)
                    b0, taken, _ = wait_done(("back", g, i))
                    tiles = slice(2 * g, 2 * g + 2)
                    if i == NB - 1 and N > NB * BLK:
                        rest = N - NB * BLK
                        one = cols(C_ONE, 2 * rest).rearrange("p (t c) -> p t c", t=2)
                        nc.vector.tensor_tensor(mix_hi[:, tiles, NB * BLK:N], one, one, ALU.subtract).then_inc(rest_done, 1)
                        nc.vector.tensor_tensor(mix_lo[:, tiles, NB * BLK:N], one, one, ALU.subtract).then_inc(rest_done, 1)
                    nc.vector.tensor_tensor(mix_lo[:, tiles, block_of(i)],
                                            bank(b0, 2 * BLK).rearrange("p (t q) -> p t q", t=2),
                                            mix_hi[:, tiles, block_of(i)].bitcast(F32), ALU.subtract).then_inc(taken, 1)

                def gla_att(c):
                    b0, taken, _ = wait_done(("gla_att", c))
                    if c >= 2:
                        wait_done(("gla_out", c - 2))
                    tri = cols(C_TRI, BLK, slice(0, BLK)).bitcast(I32).rearrange("p (a t) -> p a t", a=1).broadcast_to([BLK, 2, BLK])
                    for a in range(2):
                        ins = nc.vector.copy_predicated(att[:, c % 2, a], tri, bank(b0 + a, 2 * BLK, slice(0, BLK))
                                                        .rearrange("p (h t) -> p h t", h=2))
                    ins.then_inc(taken, 1)

                def gla_kv(c):
                    b0, taken, n = wait_done(("gla_kv", c))
                    if c:
                        wait_done(("gla_out", c - 1))
                    dve.wait_ge(decay_exp, 1)
                    new, old = state[:, c % 2], state[:, (c - 1) % 2]
                    for hh in range(2):
                        r = head_rows(hh)
                        kv = ps[r, b0 * 512:(b0 + 1) * 512].rearrange("p (t e) -> p t e", t=2)[:, :, hh * 128:(hh + 1) * 128]
                        if c == 0:
                            ins = nc.vector.tensor_copy(new[r], kv)
                        else:
                            ins = nc.vector.tensor_tensor(new[r], old[r], kv, ALU.add)
                        if hh == 0:
                            chain(ins)
                    ins.then_inc(taken, 1)
                    dve.wait_ge(taken, n)
                    nc.vector.tensor_tensor(new, new, coef[:, :, c:c + 1].broadcast_to([128, 2, 128]),
                                            ALU.mult).then_inc(state_ready, 1)
                    dve.wait_ge(state_ready, c + 1)

                def silu(hd):
                    dve.wait_ge(sigmoid_ready, hd + 1)
                    dve.wait_ge(feat_ready, 2 * (GG + hd) + 2)
                    nc.vector.tensor_tensor(feat[:, place(GG + hd)], feat[:, place(GG + hd)], xnb[:, hd % 2], ALU.mult).then_inc(silu_done, 1)

                def gla_mix(hd):
                    dve.wait_ge(silu_done, 4)
                    nc.vector.tensor_tensor(feat[:, place(GG + hd)], feat[:, place(GV + hd)], feat[:, place(GG + hd)], ALU.mult).then_inc(gla_mixed, 1)
                    dve.wait_ge(gla_mixed, hd + 1)
                    dve.wait_ge(gla_hi, hd + 1)
                    nc.vector.tensor_tensor(mix_lo[:, 4 + hd], feat[:, place(GG + hd)], mix_hi[:, 4 + hd].bitcast(F32),
                                            ALU.subtract).then_inc(gla_split, 1)

                do = dict(proj=proj, norm=norm, rope=rope, gate_log=gate_log, fox_log=fox_log, decays=decays, index=index, topk=topk,
                          select=select, logits=logits, scale=scale, mixed=mixed, gla_att=gla_att, gla_kv=gla_kv,
                          silu=silu, gla_mix=gla_mix)
                for step in STEPS:
                    if step[0] in do:
                        do[step[0]](*step[1:])

                chain(nc.vector.memset(rstd[:], 0.0))
                for m in range(KT):
                    dve.wait_ge(half_done, half0 + 2 * (U_OUT + m + 1))
                    nc.vector.tensor_tensor(halves(h[:, m]), two_banks(2 * (m % 2)), halves(h[:, m]), ALU.add).then_inc(acc_free, 1)
                    dve.wait_ge(acc_free, 2 + m + 1)
                    x_low(m, par[:, P_FFN + m:P_FFN + m + 1], l * (2 * KT) + (KT + m))
                    dve.wait_ge(sq_ready, len(SQUARES) + m + 1)
                    if m:
                        dve.wait_ge(summed, m)
                    nc.vector.tensor_tensor(rstd[:], rstd[:], sqb[:, m % 2], ALU.add).then_inc(summed, 1)
                dve.wait_ge(rstd_ready, 2)
                with dve.Fori(0, MF // 2) as j:
                    for b in range(2):
                        dve.wait_ge(half_done, half0 + j * 8 + (2 * U_GU + 4 * b + 2))
                        nc.vector.tensor_tensor(halves(sg[:, b]), two_banks(4 * b), halves(rstd[:]),
                                                ALU.mult).then_inc(gate_scaled, 1)
                        dve.wait_ge(half_done, half0 + j * 8 + (2 * U_GU + 4 * b + 4))
                        nc.vector.tensor_tensor(halves(hid[:, b]), two_banks(4 * b + 2), halves(rstd[:]),
                                                ALU.mult).then_inc(acc_free, 1)
                        dve.wait_ge(acc_free, j * 2 + (2 + N_OUT + b + 1))
                        dve.wait_ge(sg_ready, j * 2 + (b + 1))
                        nc.vector.tensor_tensor(hid[:, b], hid[:, b], sg[:, b], ALU.mult).then_inc(hidden, 1)
                        dve.wait_ge(hhi_ready, j * 2 + (b + 1))
                        nc.vector.tensor_tensor(hlo[:, bass.ds(j * 2 + b, 1), :].rearrange("p a t -> p (a t)"), hid[:, b],
                                                hhi[:, bass.ds(j * 2 + b, 1), :].rearrange("p a t -> p (a t)").bitcast(F32),
                                                ALU.subtract).then_inc(hid_ready, 1)

                chain(nc.vector.memset(rstd[:], 0.0))
                for m in range(KT):
                    dve.wait_ge(half_done, half0 + 2 * (U_DN + 3 * (m + 1)))
                    nc.vector.tensor_tensor(halves(h[:, m]), two_banks(2 * (m % 2)), halves(h[:, m]), ALU.add).then_inc(acc_free, 1)
                    dve.wait_ge(acc_free, 2 + N_OUT + MF + m + 1)
                    x_low(m, par[:, P_NEXT + m:P_NEXT + m + 1], l * (2 * KT) + (2 * KT + m))
                    dve.wait_ge(sq_ready, len(SQUARES) + KT + m + 1)
                    dve.wait_ge(h_done, l * KT + (KT + m))
                    nc.vector.tensor_tensor(rstd[:], rstd[:], sqb[:, m % 2], ALU.add).then_inc(h_done, 1)
                dve.drain().then_inc(engines_done, 1)
                dve.wait_ge(engines_done, 3)
                dve.sem_clear(layer_sems)
                dve.drain().then_inc(layer_open, 1)


def pack_columns(w):
    k, n = w.shape
    return w.reshape(k // 128, 128, n // 128, 128).transpose(2, 1, 0, 3).reshape(n // 128, 128, k)


def lay_out_weights(w_in, w_out, w_gate_up, w_down):
    edges = np.cumsum([0, 256, 64, 64, 256, 4, 64, 256, 256, 256, 4, 256, 256, 512, 512, 16])
    names = ("dq", "dk", "dv", "iq", "iw", "ik", "fq", "fk", "fv", "ff", "gq", "gk", "gv", "gg", "lr")
    at = {n: slice(edges[i], edges[i + 1]) for i, n in enumerate(names)}
    stream = np.zeros((STREAM, 128, D), w_in.dtype)
    out = stream[:DEPTH * UNITS].reshape(DEPTH, UNITS, 128, D)
    for l in range(DEPTH):
        small = np.zeros((D, 128), w_in.dtype)
        for name, row in (("dv", ROW_DV), ("lr", ROW_LR), ("ff", ROW_FF), ("iw", ROW_IW)):
            part = w_in[l][:, at[name]]
            small[:, row:row + part.shape[1]] = part
        parts = [w_in[l][:, at[n]] for n in ("dq", "dk", "ik", "iq")] + [small]
        parts += [w_in[l][:, at[n]] for n in ("fq", "fk", "fv", "gq", "gk", "gv", "gg")]
        out[l, :N_PROJ] = pack_columns(np.concatenate(parts, axis=1))
        out[l, U_OUT:U_GU] = pack_columns(w_out[l])
        out[l, U_GU:U_DN:2] = pack_columns(w_gate_up[l][:, :FF])
        out[l, U_GU + 1:U_DN:2] = pack_columns(w_gate_up[l][:, FF:])
        down = pack_columns(w_down[l])
        for s, kts in enumerate(DN_PARTS):
            a = sum(DN_PARTS[:s]) * 128
            out[l, U_DN + s::3, :, :kts * 128] = down[:, :, a:a + kts * 128]
    return stream


def lay_out_params(attn_norm, ffn_norm, dsa_q_norm, dsa_k_norm, fox_q_norm, fox_k_norm, fox_f_bias, gla_gate_w2,
                   gla_gate_b, gla_out_norm):
    p = np.zeros((DEPTH, 128, N_PAR), attn_norm.dtype)
    for l in range(DEPTH):
        p[l, :, P_ATT:P_ATT + KT] = attn_norm[l].reshape(KT, 128).T
        p[l, :, P_FFN:P_FFN + KT] = ffn_norm[l].reshape(KT, 128).T
        for c, g in ((P_DQ, dsa_q_norm), (P_DK, dsa_k_norm), (P_FQ, fox_q_norm), (P_FK, fox_k_norm)):
            p[l, :, c] = np.tile(g[l], 2)
        p[l, :, P_GO] = gla_out_norm[l]
        p[l, :, P_GB:P_GB + 2] = gla_gate_b[l].reshape(2, 128).T
        p[l, ROW_FF:ROW_FF + 4, P_FB] = fox_f_bias[l]
        p[l, ROW_LR:ROW_LR + RANK, P_W2:P_W2 + 256] = gla_gate_w2[l]
        if l:
            p[l - 1, :, P_NEXT:P_NEXT + KT] = p[l, :, P_ATT:P_ATT + KT]
    return p


def shape_constants():
    c = np.zeros((128, N_CST), np.float32)
    c[:, C_ID:C_ID + 128] = np.eye(128)
    c[:, C_ONE:C_ONE + 128] = 1
    c[:64, C_BLK:C_BLK + 64] = 1
    c[64:, C_BLK + 64:C_BLK + 128] = 1
    half = 8
    inv = np.power(np.float32(500000.0), -np.arange(half, dtype=np.float32) * np.float32(2.0) / np.float32(16))
    ang = np.arange(N, dtype=np.float32)[None, :] * inv.astype(np.float32)[:, None]
    c[:, C_COS:C_COS + N] = 1
    for base in (0, 64):
        for j in range(half):
            lo, hi = base + j, base + half + j
            c[hi, C_ROT + lo] = -1
            c[lo, C_ROT + hi] = 1
            for r in (lo, hi):
                c[r, C_COS:C_COS + N] = np.cos(ang[j])
                c[r, C_SIN:C_SIN + N] = np.sin(ang[j])
    c[:, C_RST:C_RST + N] = np.arange(N) % BLK != 0
    q = np.arange(BLK)
    c[:BLK, C_CAU:C_CAU + BLK] = np.where(q[None, :] > q[:, None], NEG, 0)
    c[:BLK, C_TRI:C_TRI + BLK] = q[None, :] >= q[:, None]
    for hd in range(4):
        for row in (32, 64, ROW_FF):
            c[row + hd, C_SEL + hd] = -8
    c[:, C_EPS] = EPS
    return c


def kernel(x, meta_tokens, attn_norm, w_in, dsa_q_norm, dsa_k_norm, fox_q_norm, fox_k_norm, fox_f_bias, gla_gate_w2,
           gla_gate_b, gla_out_norm, w_out, ffn_norm, w_gate_up, w_down):
    import concourse.bacc as bacc
    from concourse.bass_utils import run_bass_kernel_spmd

    a = np.asarray
    padding = np.zeros((N - META - SEQ, D), a(x).dtype)
    arrays = {
        "hT": np.ascontiguousarray(np.concatenate([a(meta_tokens), a(x)[0], padding], axis=0).T),
        "weights": lay_out_weights(a(w_in), a(w_out), a(w_gate_up), a(w_down)),
        "params": lay_out_params(a(attn_norm), a(ffn_norm), a(dsa_q_norm), a(dsa_k_norm), a(fox_q_norm), a(fox_k_norm),
                                 a(fox_f_bias), a(gla_gate_w2), a(gla_gate_b), a(gla_out_norm)),
        "consts": shape_constants(),
    }
    nc = bacc.Bacc("TRN2", target_bir_lowering=False, num_devices=1)
    args = [nc.dram_tensor(f"in_{n}", v.shape, mybir.dt.from_np(v.dtype), kind="ExternalInput").ap()
            for n, v in arrays.items()]
    out = nc.dram_tensor("out_hT", (D, SEQ), F32, kind="ExternalOutput").ap()
    hybrid_block(nc, *args, out)
    r = run_bass_kernel_spmd(nc, [{f"in_{n}": v for n, v in arrays.items()}], core_ids=[0])
    return np.ascontiguousarray(r.results[0]["out_hT"].T)[None]
```
